# Optimizing a Trainium2 kernel written in Bass

```python
import math
import jax, jax.numpy as jnp
from jax import lax
import numpy as np

D_MODEL = 2048
BATCH = 1
SEQ = 256
DEPTH = 2

Q_BLOCK = 128
HALF_WIDTH = D_MODEL // 2
HEAD_DIM_SB = 128
N_HEADS_SB = HALF_WIDTH // HEAD_DIM_SB
N_HEADS_DSA = 16
HEAD_DIM_DSA = HALF_WIDTH // N_HEADS_DSA
N_HEADS_IDX = 8
HEAD_DIM_IDX = 64
TOPK_MAX = 256
N_HEADS_DIL = 16
HEAD_DIM_DIL = D_MODEL // N_HEADS_DIL
DILATED_CONFIGS = ((128, 1), (512, 4), (2048, 16))
N_BUCKETS = 32
BUCKET_MAX_DIST = 2048
N_BIAS_HEADS = 16
D_FF = 4 * D_MODEL
N_EVEN = (DEPTH + 1) // 2
N_ODD = DEPTH // 2
DN_ALPHA = (2 * DEPTH) ** 0.25
DN_BETA = (8 * DEPTH) ** -0.25
LN_EPS = 1e-5
NEG = -1e30

EVEN_WIDTHS = (HALF_WIDTH, HALF_WIDTH, HALF_WIDTH,
               HALF_WIDTH, HALF_WIDTH, HALF_WIDTH,
               N_HEADS_IDX * HEAD_DIM_IDX, HEAD_DIM_IDX,
               N_HEADS_IDX)
EVEN_IN = sum(EVEN_WIDTHS)
ODD_IN = 3 * N_HEADS_DIL * HEAD_DIM_DIL

kernel_name = 'hybrid_stickbreak_dsa_dilated_deepnorm'

def layer_norm(x, g, b):
    xf = x.astype(jnp.float32)
    mu = jnp.mean(xf, axis=-1, keepdims=True)
    var = jnp.mean(jnp.square(xf - mu), axis=-1, keepdims=True)
    y = (xf - mu) * lax.rsqrt(var + LN_EPS) * g.astype(jnp.float32) + b.astype(jnp.float32)
    return y.astype(x.dtype)

def rel_bucket(dist):
    max_exact = N_BUCKETS // 2
    d_f = jnp.maximum(dist, 1).astype(jnp.float32)
    large = max_exact + (jnp.log(d_f / max_exact) / math.log(BUCKET_MAX_DIST / max_exact)
                         * (N_BUCKETS - max_exact)).astype(jnp.int32)
    large = jnp.minimum(large, N_BUCKETS - 1)
    return jnp.where(dist < max_exact, dist, large)

def stick_breaking_attention(q, k, v):
    B, S, H, dh = q.shape
    nb = S // Q_BLOCK
    qb = q.reshape(B, nb, Q_BLOCK, H, dh).transpose(1, 0, 2, 3, 4)
    s_pos = jnp.arange(S)
    scale = dh ** -0.5

    def block(args):
        qblk, n = args
        t_pos = n * Q_BLOCK + jnp.arange(Q_BLOCK)
        z = jnp.einsum('bqhe,bshe->bhqs', qblk, k).astype(jnp.float32) * scale
        strict = s_pos[None, :] < t_pos[:, None]
        log_beta = jax.nn.log_sigmoid(z)
        log_keep = jnp.where(strict, jax.nn.log_sigmoid(-z), 0.0)
        later = lax.cumsum(log_keep, axis=3, reverse=True) - log_keep
        a = jnp.where(strict, jnp.exp(log_beta + later), 0.0)
        return jnp.einsum('bhqs,bshe->bqhe', a, v.astype(jnp.float32)).astype(q.dtype)

    o = lax.map(block, (qb, jnp.arange(nb)))
    return o.transpose(1, 0, 2, 3, 4).reshape(B, S, H, dh)

def dsa_attention(q, k, v, q_idx, k_idx, w_idx, rel_bias):
    B, S, H, dh = q.shape
    nb = S // Q_BLOCK
    top_k = min(TOPK_MAX, S // 4)
    kv = jnp.concatenate([k, v], axis=-1)
    s_pos = jnp.arange(S)
    scale = dh ** -0.5
    idx_scale = HEAD_DIM_IDX ** -0.5
    w_scale = N_HEADS_IDX ** -0.5
    qb = q.reshape(B, nb, Q_BLOCK, H, dh).transpose(1, 0, 2, 3, 4)
    qib = q_idx.reshape(B, nb, Q_BLOCK, N_HEADS_IDX, HEAD_DIM_IDX).transpose(1, 0, 2, 3, 4)
    wb = w_idx.reshape(B, nb, Q_BLOCK, N_HEADS_IDX).transpose(1, 0, 2, 3)
    table = rel_bias.astype(jnp.float32)

    def block(args):
        qblk, qiblk, wblk, n = args
        t_pos = n * Q_BLOCK + jnp.arange(Q_BLOCK)
        dots = jnp.einsum('bqhe,bse->bqhs', qiblk, k_idx).astype(jnp.float32) * idx_scale
        score = jnp.einsum('bqhs,bqh->bqs', jax.nn.relu(dots), wblk.astype(jnp.float32) * w_scale)
        causal = s_pos[None, :] <= t_pos[:, None]
        score = jnp.where(causal[None], score, NEG)
        _, sel = lax.top_k(score, top_k)
        valid = sel <= t_pos[None, :, None]
        kv_sel = jax.vmap(lambda kvb, ib: kvb[ib])(kv, sel)
        k_sel, v_sel = jnp.split(kv_sel, 2, axis=-1)
        logits = jnp.einsum('bqhe,bqkhe->bhqk', qblk, k_sel).astype(jnp.float32) * scale
        dist = jnp.maximum(t_pos[None, :, None] - sel, 0)
        logits = logits + table[rel_bucket(dist)].transpose(0, 3, 1, 2)
        logits = jnp.where(valid[:, None], logits, NEG)
        p = jax.nn.softmax(logits, axis=-1)
        return jnp.einsum('bhqk,bqkhe->bqhe', p, v_sel.astype(jnp.float32)).astype(q.dtype)

    o = lax.map(block, (qb, qib, wb, jnp.arange(nb)))
    return o.transpose(1, 0, 2, 3, 4).reshape(B, S, H, dh)

def dilated_branch(q, k, v, rel_bias, window, dilation):
    B, S, H, dh = q.shape
    span = window // dilation
    chunk = dilation * Q_BLOCK
    Sp = -(-S // chunk) * chunk
    pad = Sp - S
    M = Sp // dilation
    nblk = M // Q_BLOCK

    def to_sub(a):
        a = jnp.pad(a, ((0, 0), (0, pad), (0, 0), (0, 0)))
        a = a.reshape(B, M, dilation, H, dh).transpose(0, 2, 1, 3, 4)
        return a.reshape(B, dilation, nblk, Q_BLOCK, H, dh)

    def with_prev(a):
        prev = jnp.pad(a, ((0, 0), (0, 0), (1, 0), (0, 0), (0, 0), (0, 0)))[:, :, :-1]
        return jnp.concatenate([prev, a], axis=3)

    qs = to_sub(q)
    kk = with_prev(to_sub(k))
    vv = with_prev(to_sub(v))
    logits = jnp.einsum('brnqhe,brnkhe->brnhqk', qs, kk).astype(jnp.float32) * (dh ** -0.5)
    i = jnp.arange(Q_BLOCK)[:, None]
    c = jnp.arange(2 * Q_BLOCK)[None, :]
    j = Q_BLOCK + i - c
    band = (j >= 0) & (j <= span)
    valid = band[None] & ((jnp.arange(nblk)[:, None, None] > 0) | (c >= Q_BLOCK)[None])
    bias = rel_bias.astype(jnp.float32)[rel_bucket(jnp.maximum(j, 0) * dilation)]
    logits = logits + bias.transpose(2, 0, 1)
    logits = jnp.where(valid[:, None], logits, NEG)
    m = jnp.max(logits, axis=-1, keepdims=True)
    e = jnp.exp(logits - m)
    s = jnp.sum(e, axis=-1)
    o = jnp.einsum('brnhqk,brnkhe->brnqhe', e, vv.astype(jnp.float32))
    o = o / s.transpose(0, 1, 2, 4, 3)[..., None]
    o = o.reshape(B, dilation, M, H, dh).transpose(0, 2, 1, 3, 4).reshape(B, Sp, H, dh)[:, :S]

    def stat_back(a):
        a = a.transpose(0, 1, 2, 4, 3).reshape(B, dilation, M, H)
        return a.transpose(0, 2, 1, 3).reshape(B, Sp, H)[:, :S]

    return o, stat_back(m[..., 0]), stat_back(s)

def dilated_attention(q, k, v, rel_bias):
    outs, maxes, dens = [], [], []
    for window, dilation in DILATED_CONFIGS:
        o, m, s = dilated_branch(q, k, v, rel_bias, window, dilation)
        outs.append(o)
        maxes.append(m)
        dens.append(s)
    o = jnp.stack(outs)
    m = jnp.stack(maxes)
    s = jnp.stack(dens)
    w = s * jnp.exp(m - jnp.max(m, axis=0, keepdims=True))
    out = jnp.sum(w[..., None] * o, axis=0) / jnp.sum(w, axis=0)[..., None]
    return out.astype(q.dtype)

def even_mixer(x, w_in, w_out, rel_bias):
    B, S, _ = x.shape
    h = x @ w_in
    offsets = [int(o) for o in np.cumsum(EVEN_WIDTHS)[:-1]]
    qa, ka, va, qb, kb, vb, qi, ki, wi = jnp.split(h, offsets, axis=-1)
    sb_shape = (B, S, N_HEADS_SB, HEAD_DIM_SB)
    dsa_shape = (B, S, N_HEADS_DSA, HEAD_DIM_DSA)
    oa = stick_breaking_attention(qa.reshape(sb_shape), ka.reshape(sb_shape), va.reshape(sb_shape))
    ob = dsa_attention(qb.reshape(dsa_shape), kb.reshape(dsa_shape), vb.reshape(dsa_shape),
                       qi.reshape(B, S, N_HEADS_IDX, HEAD_DIM_IDX), ki, wi, rel_bias)
    o = jnp.concatenate([oa.reshape(B, S, HALF_WIDTH), ob.reshape(B, S, HALF_WIDTH)], axis=-1)
    return o @ w_out

def odd_mixer(x, w_in, w_out, rel_bias):
    B, S, _ = x.shape
    q, k, v = jnp.split(x @ w_in, 3, axis=-1)
    shp = (B, S, N_HEADS_DIL, HEAD_DIM_DIL)
    o = dilated_attention(q.reshape(shp), k.reshape(shp), v.reshape(shp), rel_bias)
    return o.reshape(B, S, N_HEADS_DIL * HEAD_DIM_DIL) @ w_out

def sqrelu_mlp(x, w1, w2):
    return jnp.square(jax.nn.relu(x @ w1)) @ w2

def setup_inputs(seed: int = 0) -> dict:
    key = jax.random.key(seed)
    ks = jax.random.split(key, 12)
    f32 = jnp.float32
    even_scale = np.concatenate([
        np.ones(2 * HALF_WIDTH), np.full(HALF_WIDTH, DN_BETA),
        np.ones(2 * HALF_WIDTH), np.full(HALF_WIDTH, DN_BETA),
        np.ones(N_HEADS_IDX * HEAD_DIM_IDX + HEAD_DIM_IDX + N_HEADS_IDX)]).astype(np.float32)
    odd_scale = np.concatenate([np.ones(2 * D_MODEL), np.full(D_MODEL, DN_BETA)]).astype(np.float32)
    x = jax.random.normal(ks[0], (BATCH, SEQ, D_MODEL), f32)
    even_w_in = jax.random.normal(ks[1], (N_EVEN, D_MODEL, EVEN_IN), f32) * (D_MODEL ** -0.5) * jnp.asarray(even_scale)
    even_w_out = jax.random.normal(ks[2], (N_EVEN, 2 * HALF_WIDTH, D_MODEL), f32) * ((2 * HALF_WIDTH) ** -0.5 * DN_BETA)
    odd_w_in = jax.random.normal(ks[3], (N_ODD, D_MODEL, ODD_IN), f32) * (D_MODEL ** -0.5) * jnp.asarray(odd_scale)
    odd_w_out = jax.random.normal(ks[4], (N_ODD, D_MODEL, D_MODEL), f32) * (D_MODEL ** -0.5 * DN_BETA)
    rel_bias = jax.random.normal(ks[5], (N_BUCKETS, N_BIAS_HEADS), f32) * 0.5
    ln_mix_g = 1.0 + 0.05 * jax.random.normal(ks[6], (DEPTH, D_MODEL), f32)
    ln_mix_b = 0.02 * jax.random.normal(ks[7], (DEPTH, D_MODEL), f32)
    ffn_w1 = jax.random.normal(ks[8], (DEPTH, D_MODEL, D_FF), f32) * (D_MODEL ** -0.5 * DN_BETA)
    ffn_w2 = jax.random.normal(ks[9], (DEPTH, D_FF, D_MODEL), f32) * (D_FF ** -0.5 * DN_BETA)
    ln_ffn_g = 1.0 + 0.05 * jax.random.normal(ks[10], (DEPTH, D_MODEL), f32)
    ln_ffn_b = 0.02 * jax.random.normal(ks[11], (DEPTH, D_MODEL), f32)
    return {'x': x, 'even_w_in': even_w_in, 'even_w_out': even_w_out,
            'odd_w_in': odd_w_in, 'odd_w_out': odd_w_out, 'rel_bias': rel_bias,
            'ln_mix_g': ln_mix_g, 'ln_mix_b': ln_mix_b, 'ffn_w1': ffn_w1, 'ffn_w2': ffn_w2,
            'ln_ffn_g': ln_ffn_g, 'ln_ffn_b': ln_ffn_b}

def reference(x, even_w_in, even_w_out, odd_w_in, odd_w_out, rel_bias,
              ln_mix_g, ln_mix_b, ffn_w1, ffn_w2, ln_ffn_g, ln_ffn_b):
    for layer in range(DEPTH):
        if layer % 2 == 0:
            mix = even_mixer(x, even_w_in[layer // 2], even_w_out[layer // 2], rel_bias)
        else:
            mix = odd_mixer(x, odd_w_in[layer // 2], odd_w_out[layer // 2], rel_bias)
        x = layer_norm(DN_ALPHA * x + mix, ln_mix_g[layer], ln_mix_b[layer])
        x = layer_norm(DN_ALPHA * x + sqrelu_mlp(x, ffn_w1[layer], ffn_w2[layer]),
                       ln_ffn_g[layer], ln_ffn_b[layer])
    return x


_drawn_inputs = setup_inputs


def setup_inputs(seed=0):
    import zlib

    import numpy as np

    out = dict(_drawn_inputs(seed))
    spreads = {}
    factors = {'rel_bias': 2.79}
    for name, (base, spread) in spreads.items():
        noise = np.random.default_rng([zlib.crc32(name.encode()), seed]).standard_normal(out[name].shape)
        drawn = base * np.exp(spread * noise) if base else spread * noise
        out[name] = __import__('jax').numpy.asarray(drawn.astype(out[name].dtype))
    for name, factor in factors.items():
        out[name] = (out[name] * factor).astype(out[name].dtype)
    return out
```

```python
from contextlib import ExitStack

import concourse.bass as bass
import numpy as np
from concourse import mybir

ALU = mybir.AluOpType
ACT = mybir.ActivationFunctionType
F32 = mybir.dt.float32
F32R = mybir.dt.float32r

P = 128
SEQ = 256
D = 2048
MT = SEQ // P
KB = D // P
NC = 512
G = 2
TPC = KB // G
RAW = 8
SPL = 4
HALF = D // 2
DH = 128
DS = 64
N_IDX = 8
TOPK = min(256, SEQ // 4)
D_FF = 4 * D
DEPTH = 2
ALPHA = (2 * DEPTH) ** 0.25
LN_EPS = 1e-5
NEG = -1e30
LOWEST = -3e38
N_BUCKETS = 32
BUCKET_MAX_DIST = 2048
CONFIGS = ((128, 1), (512, 4), (2048, 16))
SC = P + SEQ
OFF = 2 * SEQ - 1

SB, DSA, DIL = "stick-breaking", "sparse", "dilated"


def head_schedule(even):
    heads = []
    if even:
        for g in range(2):
            k_end = 16 + 24 * g + 15
            for i in range(8):
                n = 8 * g + i
                heads.append((DSA, g % 2, i, n, HALF // P + n // 2, (n % 2) * DS, k_end + 6 + 3 * i))
        for g in range(2, 4):
            k_end = 16 + 24 * g + 15
            for i in range(4):
                heads.append((SB, g % 2, i, None, 4 * (g - 2) + i, 0, k_end + 6 + (3 if g == 3 else 6) * i))
    else:
        for g in range(4):
            k_end = 24 * g + 15
            for i in range(4):
                n = 4 * g + i
                heads.append((DIL, g % 2, i, n, n, 0, k_end + 6 + (2 if g == 3 else 6) * i))
    return heads


def mixer_plan(even):
    chunks = []
    if even:
        chunks += [("qi", 6 * HALF, NC), ("ki", 6 * HALF + N_IDX * DS, DS + N_IDX)]
        starts = [(3 * HALF, c) for c in range(2)] + [(0, c) for c in range(2)]
        for base, c in starts:
            chunks += [(n, base + i * HALF + c * NC, NC) for i, n in enumerate("qkv")]
        late = [0, 1, 4, 5, 6, 7, 2, 3]
    else:
        for c in range(4):
            chunks += [(n, i * D + c * NC, NC) for i, n in enumerate("qkv")]
        late = list(range(8))
    slots = [
        (what, n, col, width, t, t == 0, t == TPC - 1)
        for n, (what, col, width) in enumerate(chunks)
        for t in range(TPC)
    ]
    n_in = len(chunks)
    order = [(0, t) for t in range(6)] + [(1, t) for t in range(6)]
    order += [(0, 6), (0, 7), (1, 6), (1, 7)] + [(c, t) for c in (2, 3) for t in range(8)]
    slots += [("out", n_in + c, c * NC, NC, late[t], t == 0, t == TPC - 1) for c, t in order]
    return slots, n_in


def hybrid_trunk(nc, x, even_w_in, even_w_out, odd_w_in, odd_w_out, rel_bias,
                 ln_mix_g, ln_mix_b, ffn_w1, ffn_w2, ln_ffn_g, ln_ffn_b,
                 bucket_rows, branch_count, out):
    with ExitStack() as ctx:
        top = [(nc.sbuf_base + 63) // 64 * 64]

        def sb(name, shape, dt=F32, at=None):
            offset = top[0] if at is None else at
            size = 4 * int(np.prod(shape[1:]))
            if at is None:
                top[0] = offset + (size + 63) // 64 * 64
            return nc.alloc_sbuf_tensor_at(name, shape, dt, offset=offset)

        def sem(name):
            return ctx.enter_context(nc.semaphore(name))

        X = sb("X", [P, MT, D])
        XTh, XTl = sb("XTh", [P, KB, SEQ], F32R), sb("XTl", [P, KB, SEQ], F32R)
        HTh, HTl = sb("HTh", [P, KB, SEQ], F32R), sb("HTl", [P, KB, SEQ], F32R)
        raw = [sb(f"raw{i}", [P, G, NC]) for i in range(RAW)]
        whi = [sb(f"whi{i}", [P, G, NC], F32R) for i in range(SPL)]
        wlo = [sb(f"wlo{i}", [P, G, NC], F32R) for i in range(SPL)]
        group_at = top[0]
        qT = [sb(f"qT{i}", [P, 4, SEQ]) for i in range(2)]
        kT = [sb(f"kT{i}", [P, 4, SEQ]) for i in range(2)]
        v = [sb(f"v{i}", [P, MT, NC]) for i in range(2)]
        gain = sb("gain", [P, D], at=group_at)
        shift = sb("shift", [P, D], at=group_at + 4 * D)
        stage = sb("stage", [P, MT, NC])
        squared = sb("squared", [P, MT, NC])
        qiT = sb("qiT", [P, 4, SEQ])
        kiT = sb("kiT", [P, SEQ])
        ki2 = sb("ki2", [P, MT, 2 * DS])
        wi = sb("wi", [P, MT, N_IDX])
        relu_dots = sb("relu_dots", [P, NC])
        score = sb("score", [P, SC])
        work = sb("work", [P, SC])
        top8 = sb("top8", [P, MT, 8])
        unpicked = sb("unpicked", [P, SC], F32R)
        bias = [sb(f"bias{i}", [P, SC]) for i in range(2)]
        logit = [sb(f"logit{i}", [P, SC]) for i in range(2)]
        prob = [sb(f"prob{i}", [P, SC]) for i in range(2)]
        probT = sb("probT", [P, SC])
        row_max = sb("row_max", [P, MT])
        neg_max = sb("neg_max", [P, MT])
        den = sb("den", [P, 2, MT])
        rden = sb("rden", [P, MT])
        stats = sb("stats", [P, MT, 4, 6])
        mean_var = sb("mean_var", [P, MT, 2])
        var_eps = sb("var_eps", [P, MT])
        minus_half = sb("minus_half", [P, MT])
        rstd = sb("rstd", [P, MT])
        shift_mean = sb("shift_mean", [P, MT])
        ident = sb("ident", [P, P])
        neg_identr = sb("neg_identr", [P, P], F32R)
        not_before = sb("not_before", [P, P])
        not_before_r = sb("not_before_r", [P, P], F32R)
        neg_suffix = sb("neg_suffix", [P, P])
        neg_ones = sb("neg_ones", [P, P])
        counts = sb("counts", [P, SC])
        table = sb("table", [N_BUCKETS + 1, 16])
        bucket_sb = sb("bucket_sb", [N_BUCKETS + 1, 2, OFF], at=group_at)
        bias_rows = sb("bias_rows", [16, 2, OFF + 1], at=group_at + 8 * (OFF + 1))
        assert top[0] <= nc.sbuf_usable_end, top[0]
        rows_dram = nc.dram_tensor("bias_rows_dram", [16, 2, P, OFF + 1], F32, kind="Internal")

        ps = [ctx.enter_context(nc.psum_tensor(f"ps{i}", [P, MT, NC], F32)) for i in range(2)]
        ps_dots = ctx.enter_context(nc.psum_tensor("ps_dots", [P, NC], F32))
        ps_probT = ctx.enter_context(nc.psum_tensor("ps_probT", [P, NC], F32))
        ps_turn = ctx.enter_context(nc.psum_tensor("ps_turn", [P, NC], F32))
        ps_out = ctx.enter_context(nc.psum_tensor("ps_out", [P, NC], F32))

        s_x = sem("x_loaded")
        s_const_in = sem("constants_loaded")
        s_one = sem("ones_row_built")
        s_const = sem("constants_built")
        s_constr = sem("constants_rounded")
        s_rows = sem("bias_rows_computed")
        s_rows_sb = sem("bias_rows_copied")
        s_rows_dram = sem("bias_rows_in_dram")
        s_raw = [sem(f"raw_loaded{i}") for i in range(RAW)]
        s_hi = sem("weights_high")
        s_lo = sem("weights_low")
        s_mm = sem("tile_multiplied")
        s_stage = sem("chunk_staged")
        s_square = sem("chunk_squared")
        s_v = sem("v_ready")
        s_ki2 = sem("indexer_key_staged")
        s_added = sem("chunk_added")
        s_stat = sem("chunk_statistics")
        s_turn = sem("blocks_transposed")
        s_turn_hi = sem("blocks_high")
        s_turned = sem("blocks_taken")
        s_gain = sem("gain_loaded")
        s_aggr = sem("mean_variance")
        s_var = sem("variance_guarded")
        s_rstd = sem("rstd_ready")
        s_centre = sem("centre_ready")
        s_centred = sem("block_centred")
        s_gained = sem("block_gained")
        s_shifted = sem("block_shifted")
        s_alpha = sem("residual_scaled")
        s_dots = sem("indexer_dots")
        s_relu = sem("indexer_relu")
        s_score = sem("score_terms")
        s_causal = sem("score_masked")
        s_top = sem("topk_steps")
        s_pick = sem("selection_ready")
        s_bias = [sem(f"bias_loaded{i}") for i in range(2)]
        s_logits = sem("head_dots")
        s_max = sem("row_max_ready")
        s_nmax = sem("neg_max_ready")
        s_exp = sem("exponentials")
        s_den = sem("denominator_ready")
        s_rden = sem("reciprocal_ready")
        s_prob = sem("probabilities")
        s_probT = sem("prob_transposed")
        s_stick = sem("stick_steps")
        s_keep = sem("stick_softplus")
        s_later = sem("stick_cumsum")
        s_right = sem("right_operand")
        s_pv = sem("head_output")
        s_ohi = sem("head_output_high")
        s_olo = sem("head_output_low")
        s_store = sem("output_stored")

        plans = [mixer_plan(True), mixer_plan(False)]
        heads = [head_schedule(True), head_schedule(False)]
        H0 = [0, len(heads[0])]
        T0, V0, U0, B0 = [0], [0], [0], [0]
        for layer in range(DEPTH):
            plan, n_in = plans[layer]
            staged = sum(last and what in ("qi", "q", "k") for what, _, _, _, _, _, last in plan)
            mixer = (len(plan), 4, 8 + 2 * staged + (layer == 0), staged)
            mlp = (32 * TPC, 16, 8 + 32, 16)
            for tiles, adds, pairs, stages in (mixer, mlp):
                T0.append(T0[-1] + tiles)
                V0.append(V0[-1] + adds)
                U0.append(U0[-1] + pairs)
                B0.append(B0[-1] + stages)
        N_T = T0[-1]
        all_heads = heads[0] + heads[1]
        soft = [h for h, head in enumerate(all_heads) if head[0] != SB]
        stick = [h for h, head in enumerate(all_heads) if head[0] == SB]
        dilated = [h for h, head in enumerate(all_heads) if head[0] == DIL]

        turns, takes, leaves, ends = [{}, {}], [{}, {}], [{}, {}], [{}, {}]
        turn_no, stage_no, v_no, stage_free = [{}, {}], [{}, {}], [{}, {}], [{}, {}]
        for layer in range(DEPTH):
            turn, staged, free = U0[2 * layer] + 8, B0[2 * layer], None
            for slot, (what, chunk, _, _, _, _, last) in enumerate(plans[layer][0]):
                if last:
                    ends[layer][chunk] = slot
                if not last or what == "out":
                    continue
                leaves[layer][slot + 4] = (what, chunk)
                if what == "v":
                    v_no[layer][chunk] = sum(map(len, v_no))
                    continue
                for pair in range(1 if what == "ki" else 2):
                    turns[layer][slot + 2 + 2 * pair] = (what, chunk, pair)
                    takes[layer][slot + 6 + 2 * pair] = (what, chunk, pair)
                    turn_no[layer][(chunk, pair)] = turn
                    turn += 1
                if what != "ki":
                    stage_no[layer][chunk] = staged
                    stage_free[layer][chunk] = free
                    free = turn
                    staged += 1
        turn_ki = turn_no[0][(1, 0)]
        idx_lead = 2
        dots_after = {19 + u: u for u in range(6)}
        dots_heads = [(0, 2, 4, 6), (1, 3, 5, 7), (0, 2), (4, 6), (1, 3), (5, 7)]
        dots_tile = [0, 0, 1, 1, 1, 1]
        topk_at = {29 + r: r for r in range(TOPK // 8)}

        def group_of(layer, chunk):
            return (chunk - (idx_lead if layer == 0 else 0)) // 3

        def chunk_of(layer, group, what):
            return 3 * group + "qkv".index(what) + (idx_lead if layer == 0 else 0)

        def heads_before(layer, group):
            per = [8, 8, 4, 4] if layer == 0 else [4] * 4
            return H0[layer] + sum(per[:group + 1])

        def group_head(layer, n):
            per = [8, 8, 4, 4] if layer == 0 else [4] * 4
            return next(g for g in range(4) if n < sum(per[:g + 1]))

        def keys(m):
            return slice(0, P) if m == 0 else slice(P, SC)

        def stick_bank(h):
            return (ps_dots, ps_probT)[stick.index(h) % 2]

        block = ctx.enter_context(nc.Block())

        @block.sync
        def _(sp):
            for m in range(MT):
                sp.dma_start(X[:, m, :], x[0, m * P:(m + 1) * P, :]).then_inc(s_x, 16)

            def load(w, tile, j, row, col, width=NC):
                if not (isinstance(tile, int) and tile < RAW):
                    sp.wait_ge(s_lo, tile - RAW + 1)
                src = w[bass.ds(row, G * P), bass.ds(col, width)].rearrange("(g p) n -> p g n", p=P)
                sp.dma_start(raw[j % RAW][:, :, 0:width], src).then_inc(s_raw[j % RAW], 16)

            for layer in range(DEPTH):
                w_in = even_w_in[0] if layer == 0 else odd_w_in[0]
                w_out = even_w_out[0] if layer == 0 else odd_w_out[0]
                for slot, (what, chunk, col, width, t, _, _) in enumerate(plans[layer][0]):
                    load(w_out if what == "out" else w_in, T0[2 * layer] + slot, slot, t * G * P, col, width)

                def quarter(q):
                    for c in range(8):
                        for t in range(TPC):
                            tile = q * (8 * TPC) + (T0[2 * layer + 1] + c * TPC + t)
                            if c < 4:
                                load(ffn_w1[layer], tile, t, t * G * P, q * D + c * NC)
                            else:
                                load(ffn_w2[layer], tile, t, q * D + t * G * P, (c - 4) * NC)

                quarter(0)
                with sp.Fori(1, 4) as q:
                    quarter(q)

        @block.gpsimd
        def _(pool):
            pool.dma_start(bucket_sb[:], bucket_rows).then_inc(s_const_in, 16)
            pool.dma_start(table[0:N_BUCKETS, :], rel_bias).then_inc(s_const_in, 16)
            pool.dma_start(counts[:], branch_count).then_inc(s_const_in, 16)
            pool.memset(ident[:], 0.0).then_inc(s_const, 1)
            pool.memset(not_before[:], 0.0).then_inc(s_const, 1)
            pool.memset(neg_suffix[:], -1.0).then_inc(s_const, 1)
            pool.memset(neg_ones[:], -1.0).then_inc(s_const, 1)
            pool.memset(minus_half[:], -0.5).then_inc(s_const, 1)
            pool.wait_ge(s_const, 5)
            pool.affine_select(out=ident[:], in_=ident[:], compare_op=ALU.not_equal, fill=1.0, base=0,
                               pattern=[[-1, P]], channel_multiplier=1).then_inc(s_const, 1)
            pool.affine_select(out=not_before[:], in_=not_before[:], compare_op=ALU.is_gt, fill=1.0, base=0,
                               pattern=[[1, P]], channel_multiplier=-1).then_inc(s_const, 1)
            pool.affine_select(out=neg_suffix[:], in_=neg_suffix[:], compare_op=ALU.is_ge, fill=0.0, base=0,
                               pattern=[[-1, P]], channel_multiplier=1).then_inc(s_const, 1)
            pool.wait_ge(s_rows_sb, 2)
            for k in range(2):
                copies = bass.AP(bias_rows, k * (OFF + 1), [[2 * (OFF + 1), 16], [0, P], [1, OFF]])
                pool.dma_start(rows_dram.ap()[:, k, :, 0:OFF], copies).then_inc(s_rows_dram, 16)
            pool.wait_ge(s_rows_dram, 32)

            def load_bias(h):
                kind, _, _, row, _, _, _ = all_heads[h]
                n = soft.index(h)
                if n >= 2:
                    pool.wait_ge(s_nmax, n - 1)
                start = (row * 2 + (kind == DIL)) * P * (OFF + 1) + SEQ - 1
                rows = rows_dram.ap()
                pool.dma_start(bias[n % 2][:, keys(0)], bass.AP(rows.tensor, start, [[OFF, P], [1, P]]))\
                    .then_inc(s_bias[n % 2], 16)
                pool.dma_start(bias[n % 2][:, keys(1)], bass.AP(rows.tensor, start - P, [[OFF, P], [1, SEQ]]))\
                    .then_inc(s_bias[n % 2], 16)

            def scale_residual(stage):
                for b in range(4):
                    pool.wait_ge(s_turn, U0[stage] + 2 * b + 2)
                    xb = X[:, :, b * NC:(b + 1) * NC]
                    pool.tensor_scalar(xb, xb, ALPHA, None, ALU.mult).then_inc(s_alpha, 1)

            def norm(n, gains, shifts):
                pool.dma_start(gain[:], bass.AP(gains.tensor, gains.offset, [[0, P], [1, D]])).then_inc(s_gain, 16)
                pool.dma_start(shift[:], bass.AP(shifts.tensor, shifts.offset, [[0, P], [1, D]])).then_inc(s_gain, 16)
                pool.wait_ge(s_aggr, n + 1)
                pool.tensor_scalar(var_eps[:], mean_var[:, :, 1], LN_EPS, None, ALU.add).then_inc(s_var, 1)
                pool.wait_ge(s_var, n + 1)
                pool.tensor_tensor(rstd[:], var_eps[:], minus_half[:], ALU.pow).then_inc(s_rstd, 1)
                pool.wait_ge(s_gain, 32 * (n + 1))
                for b in range(4):
                    pool.wait_ge(s_gained, 4 * n + b + 1)
                    for m in range(MT):
                        xb = X[:, m, b * NC:(b + 1) * NC]
                        last = pool.tensor_tensor(xb, xb, shift[:, b * NC:(b + 1) * NC], ALU.add)
                    last.then_inc(s_shifted, 1)

            for layer in range(DEPTH):
                scale_residual(2 * layer)
                own = [h for h in soft if H0[layer] <= h < H0[layer] + len(heads[layer])]
                for h in own[:2]:
                    load_bias(h)
                if layer == 0:
                    for m in range(MT):
                        pool.wait_ge(s_score, N_IDX * (m + 1))
                        pool.affine_select(out=score[:, keys(m)], in_=score[:, keys(m)], compare_op=ALU.is_ge,
                                           fill=NEG, base=m * P, pattern=[[-1, P * (m + 1)]],
                                           channel_multiplier=1).then_inc(s_causal, 1)
                for h in own[2:]:
                    load_bias(h)
                pool.wait_ge(s_pv, H0[layer] + len(heads[layer]))
                norm(2 * layer, ln_mix_g[layer], ln_mix_b[layer])
                scale_residual(2 * layer + 1)
                mlp = 2 * layer + 1

                def quarter(q):
                    for c in range(4):
                        pool.wait_ge(s_stage, q * 4 + (B0[mlp] + c + 1))
                        pool.wait_ge(s_turn, q * 8 + (U0[mlp] + 8 + 2 * c))
                        pool.tensor_tensor(squared[:], stage[:], stage[:], ALU.mult).then_inc(s_square, 1)

                quarter(0)
                with pool.Fori(1, 4) as q:
                    quarter(q)
                norm(mlp, ln_ffn_g[layer], ln_ffn_b[layer])
            rows = out[0].rearrange("(m p) d -> p m d", p=P)
            for b in range(4):
                pool.wait_ge(s_shifted, 4 * 3 + b + 1)
                pool.dma_start(rows[:, :, b * NC:(b + 1) * NC], X[:, :, b * NC:(b + 1) * NC]).then_inc(s_store, 16)
            pool.wait_ge(s_store, 4 * 16)

        @block.scalar
        def _(act):
            act.wait_ge(s_const, 8)
            act.activation(neg_identr[:], ident[:], ACT.Copy, scale=NEG).then_inc(s_constr, 1)
            act.activation(not_before_r[:], not_before[:], ACT.Copy).then_inc(s_constr, 1)
            act.wait_ge(s_rows, 1)
            act.activation(bias_rows[:, 0, 0:OFF], ps_dots[0:16, 0:OFF], ACT.Copy).then_inc(s_rows_sb, 1)
            act.activation(bias_rows[:, 1, 0:OFF], ps_probT[0:16, 0:OFF], ACT.Copy).then_inc(s_rows_sb, 1)

            def high(tile, lap, j, width=NC):
                act.wait_ge(s_raw[j % RAW], lap)
                if not (isinstance(tile, int) and tile < SPL):
                    act.wait_ge(s_mm, tile - SPL + 1)
                act.activation(whi[j % SPL][:, :, 0:width], raw[j % RAW][:, :, 0:width], ACT.Copy).then_inc(s_hi, 1)

            def high_at(tile, width=NC):
                high(tile, 16 * (tile // RAW + 1), tile, width)

            def turn_high(turn, bank, dst, pair):
                act.wait_ge(s_turn, turn + 1)
                act.activation(dst[:, 2 * pair:2 * pair + 2, :], bank[:].rearrange("p (b t) -> p b t", b=2),
                               ACT.Copy).then_inc(s_turn_hi, 1)

            def centre(n, b):
                if b == 0:
                    act.wait_ge(s_centre, n + 1)
                for m in range(MT):
                    xb = X[:, m, b * NC:(b + 1) * NC]
                    last = act.activation(xb, xb, ACT.Identity, bias=shift_mean[:, m:m + 1], scale=rstd[:, m:m + 1])
                last.then_inc(s_centred, 1)

            def enter(stage):
                for t in range(4):
                    high_at(T0[stage] + t)
                for b in range(4):
                    if stage:
                        centre(stage - 1, b)
                    for pair in (2 * b, 2 * b + 1):
                        turn_high(U0[stage] + pair, (ps_turn, ps_out)[pair % 2], XTh, pair)
                    if b in (1, 2):
                        high_at(T0[stage] + 2 * b + 2)
                        high_at(T0[stage] + 2 * b + 3)

            def leave(layer, what, chunk):
                act.wait_ge(s_mm, T0[2 * layer] + ends[layer][chunk] + 1)
                acc = ps[chunk % 2]
                if what == "ki":
                    for i in range(2):
                        act.activation(ki2[:, :, i * DS:(i + 1) * DS], acc[:, :, 0:DS], ACT.Copy).then_inc(s_ki2, 1)
                    act.activation(wi[:], acc[:, :, DS:DS + N_IDX], ACT.Copy, scale=N_IDX ** -0.5).then_inc(s_ki2, 1)
                elif what == "v":
                    g = group_of(layer, chunk)
                    if g >= 2:
                        act.wait_ge(s_pv, heads_before(layer, g - 2))
                    act.activation(v[g % 2][:], acc[:], ACT.Copy).then_inc(s_v, 1)
                else:
                    sparse = what == "qi" or (layer == 0 and group_of(layer, chunk) < 2)
                    scale = 1.0 if what == "k" else (DS if sparse else DH) ** -0.5
                    if stage_free[layer][chunk] is not None:
                        act.wait_ge(s_turn, stage_free[layer][chunk])
                    act.activation(stage[:], acc[:], ACT.Copy, scale=scale).then_inc(s_stage, 1)

            def relu_dots_of(u):
                act.wait_ge(s_dots, u + 1)
                if u:
                    act.wait_ge(s_score, (0, 4, 8, 10, 12, 14)[u])
                act.activation(relu_dots[:], ps_dots[:], ACT.Relu).then_inc(s_relu, 1)

            def exponentials(h):
                act.wait_ge(s_nmax, soft.index(h) + 1)
                for m in range(MT):
                    lg = logit[h % 2][:, keys(m)]
                    if all_heads[h][0] == DSA:
                        last = act.activation(lg, lg, ACT.Exp, bias=neg_max[:, m:m + 1],
                                              accum_out=den[:, h % 2, m:m + 1])
                    else:
                        last = act.activation(lg, lg, ACT.Exp, bias=neg_max[:, m:m + 1])
                last.then_inc(s_exp, 1)

            def stick_log(h):
                n = stick.index(h)
                act.wait_ge(s_logits, h + 1)
                act.wait_ge(s_right, h - 1)
                act.activation(logit[h % 2][:], stick_bank(h)[:, 0:SC], ACT.Abs).then_inc(s_stick, 1)
                act.wait_ge(s_stick, 3 * n + 1)
                act.activation(logit[h % 2][:], logit[h % 2][:], ACT.Exp, scale=-1.0).then_inc(s_stick, 1)
                act.wait_ge(s_stick, 3 * n + 2)
                act.activation(logit[h % 2][:], logit[h % 2][:], ACT.Ln, bias=1.0).then_inc(s_stick, 1)

            def right_operand(h):
                if h:
                    act.wait_ge(s_pv, h)
                if all_heads[h][0] == SB:
                    act.wait_ge(s_later, stick.index(h) + 1)
                    act.activation(probT[:], stick_bank(h)[:, 0:SC], ACT.Exp).then_inc(s_right, 1)
                else:
                    act.wait_ge(s_probT, soft.index(h) + 1)
                    act.activation(probT[:], ps_probT[:, 0:SC], ACT.Copy).then_inc(s_right, 1)

            def output_high(h):
                kind, _, _, _, blk, part, _ = all_heads[h]
                rows = slice(part, part + (DS if kind == DSA else DH))
                act.wait_ge(s_pv, h + 1)
                act.activation(HTh[rows, blk, :], ps_out[rows, 0:SEQ], ACT.Copy).then_inc(s_ohi, 1)

            for layer in range(DEPTH):
                t0 = T0[2 * layer]
                enter(2 * layer)
                for slot, (_, _, _, width, _, _, _) in enumerate(plans[layer][0]):
                    if slot >= TPC:
                        high_at(t0 + slot, width)
                    if slot in leaves[layer]:
                        leave(layer, *leaves[layer][slot])
                    if layer == 0 and slot - 4 in dots_after:
                        relu_dots_of(dots_after[slot - 4])
                    for h in range(H0[layer], H0[layer] + len(heads[layer])):
                        start = all_heads[h][6]
                        if slot == start + 4 and all_heads[h][0] == SB:
                            stick_log(h)
                        elif slot == start + 4:
                            exponentials(h)
                        elif slot == start + 7:
                            right_operand(h)
                        elif slot == start + 9:
                            output_high(h)
                mlp = 2 * layer + 1
                enter(mlp)

                def quarter(q, t0, b0, u0):
                    for c in range(8):
                        for t in range(TPC):
                            if c or not isinstance(q, int):
                                tile = q * (8 * TPC) + (t0 + c * TPC + t)
                                high(tile, q * (16 * 8) + 16 * (t0 // TPC + c + 1), t)
                            if 1 <= c <= 4 and t == 3:
                                act.wait_ge(s_mm, q * (8 * TPC) + (t0 + c * TPC))
                                act.wait_ge(s_square, q * 4 + (16 * layer + c - 1))
                                act.activation(stage[:], ps[(c - 1) % 2][:], ACT.Relu).then_inc(s_stage, 1)
                            if 1 <= c <= 4 and t in (6, 7):
                                pair = 2 * (c - 1) + t - 6
                                turn_high(q * 8 + (u0 + 8 + pair), (ps_turn, ps_out)[t - 6], HTh, pair)

                quarter(0, T0[mlp], B0[mlp], U0[mlp])
                with act.Fori(1, 4) as q:
                    quarter(q, T0[mlp], B0[mlp], U0[mlp])
            for b in range(4):
                centre(3, b)

        @block.vector
        def _(dve):
            dve.memset(table[N_BUCKETS:N_BUCKETS + 1, :], 1.0).then_inc(s_one, 1)

            def low(tile, j, width=NC):
                dve.wait_ge(s_hi, tile + 1)
                if not (isinstance(tile, int) and tile < SPL):
                    dve.wait_ge(s_mm, tile - SPL + 1)
                dve.tensor_tensor(wlo[j % SPL][:, :, 0:width], raw[j % RAW][:, :, 0:width],
                                  whi[j % SPL][:, :, 0:width].bitcast(F32), ALU.subtract).then_inc(s_lo, 1)

            def turn_low(turn, turn_hi, bank, hi, lo, pair):
                dve.wait_ge(s_turn_hi, turn_hi + 1)
                dve.tensor_tensor(lo[:, 2 * pair:2 * pair + 2, :], bank[:].rearrange("p (b t) -> p b t", b=2),
                                  hi[:, 2 * pair:2 * pair + 2, :].bitcast(F32), ALU.subtract).then_inc(s_turned, 1)

            def add(stage, n, c, done):
                dve.wait_ge(s_mm, done)
                dve.wait_ge(s_alpha, 4 * stage + 4)
                xb = X[:, :, c * NC:(c + 1) * NC]
                dve.tensor_tensor(xb, ps[c % 2][:], xb, ALU.add).then_inc(s_added, 1)

            def statistics(n, c):
                dve.wait_ge(s_added, n + 1)
                for m in range(MT):
                    last = dve.bn_stats(stats[:, m, c, :], X[:, m, c * NC:(c + 1) * NC])
                last.then_inc(s_stat, 1)

            def gained(n, b):
                dve.wait_ge(s_centred, 4 * n + b + 1)
                dve.wait_ge(s_gain, 32 * (n + 1))
                for m in range(MT):
                    xb = X[:, m, b * NC:(b + 1) * NC]
                    last = dve.tensor_tensor(xb, xb, gain[:, b * NC:(b + 1) * NC], ALU.mult)
                last.then_inc(s_gained, 1)

            def aggregate(n, adds):
                dve.wait_ge(s_stat, adds)
                for m in range(MT):
                    last = dve.bn_aggr(mean_var[:, m, :], stats[:, m, :, :])
                last.then_inc(s_aggr, 1)
                dve.wait_ge(s_rstd, n + 1)
                dve.scalar_tensor_tensor(out=shift_mean[:], in0=mean_var[:, :, 0], scalar=-1.0, in1=rstd[:],
                                         op0=ALU.mult, op1=ALU.mult).then_inc(s_centre, 1)

            def hi_count(stage):
                return sum((8, 40)[i % 2] for i in range(stage))

            def enter(stage):
                for t in range(3):
                    low(T0[stage] + t, t)
                if stage:
                    add(stage - 1, V0[stage] - 1, 3, T0[stage])
                low(T0[stage] + 3, 3)
                if stage:
                    statistics(V0[stage] - 1, 3)
                    aggregate(stage - 1, V0[stage])
                for b in range(4):
                    if stage:
                        gained(stage - 1, b)
                    for pair in (2 * b, 2 * b + 1):
                        turn_low(U0[stage] + pair, hi_count(stage) + pair, (ps_turn, ps_out)[pair % 2], XTh, XTl, pair)
                    if b in (1, 2):
                        low(T0[stage] + 2 * b + 2, 2 * b + 2)
                        low(T0[stage] + 2 * b + 3, 2 * b + 3)

            def take(layer, what, chunk, pair):
                turn = turn_no[layer][(chunk, pair)]
                dve.wait_ge(s_turn, turn + 1)
                if what == "ki":
                    dve.tensor_copy(kiT[:], ps_turn[:, 0:SEQ]).then_inc(s_turned, 1)
                    return
                if what == "qi":
                    dst = qiT
                else:
                    g = group_of(layer, chunk)
                    dst = (qT if what == "q" else kT)[g % 2]
                    if layer == 0 and g == 0:
                        dve.wait_ge(s_rows_dram, 32)
                    if g >= 2:
                        dve.wait_ge(s_logits, heads_before(layer, g - 2))
                dve.tensor_copy(dst[:, 2 * pair:2 * pair + 2, :],
                                ps_turn[:].rearrange("p (b t) -> p b t", b=2)).then_inc(s_turned, 1)

            def score_terms(u):
                m, hs = dots_tile[u], dots_heads[u]
                dve.wait_ge(s_relu, u + 1)
                dve.wait_ge(s_ki2, 3)
                width = P * (m + 1)
                for i, h in enumerate(hs):
                    n = (0, 4, 8, 10, 12, 14)[u] + i
                    term = relu_dots[:, i * width:(i + 1) * width]
                    if n % N_IDX == 0:
                        dve.tensor_scalar(score[:, keys(m)], term, wi[:, m, h:h + 1], None, ALU.mult).then_inc(s_score, 1)
                        continue
                    dve.wait_ge(s_score, n)
                    dve.scalar_tensor_tensor(out=score[:, keys(m)], in0=term, scalar=wi[:, m, h:h + 1],
                                             in1=score[:, keys(m)], op0=ALU.mult, op1=ALU.add).then_inc(s_score, 1)

            def topk_round(r):
                src = score if r == 0 else work
                if r == 0:
                    dve.wait_ge(s_causal, MT)
                else:
                    dve.wait_ge(s_top, 4 * r)
                for m in range(MT):
                    dve.max(top8[:, m, :], src[:, keys(m)]).then_inc(s_top, 1)
                for m in range(MT):
                    dve.wait_ge(s_top, 4 * r + m + 1)
                    dve.match_replace(work[:, keys(m)], top8[:, m, :], src[:, keys(m)], LOWEST).then_inc(s_top, 1)

            def selection():
                dve.wait_ge(s_top, 4 * (TOPK // 8))
                dve.tensor_tensor(unpicked[:], work[:], score[:], ALU.is_equal).then_inc(s_pick, 1)

            def logits_max(h):
                n = soft.index(h)
                dve.wait_ge(s_logits, h + 1)
                dve.wait_ge(s_bias[n % 2], 32 * (n // 2 + 1))
                if h >= 2:
                    dve.wait_ge(s_right, h - 1)
                for m in range(MT):
                    last = dve.tensor_tensor_reduce(
                        out=logit[h % 2][:, keys(m)], in0=ps_dots[:, keys(m)], in1=bias[n % 2][:, keys(m)],
                        scale=1.0, scalar=LOWEST, op0=ALU.add, op1=ALU.max, accum_out=row_max[:, m:m + 1])
                last.then_inc(s_max, 1)
                dve.wait_ge(s_max, n + 1)
                if n:
                    dve.wait_ge(s_exp, n)
                dve.tensor_scalar(neg_max[:], row_max[:], -1.0, None, ALU.mult).then_inc(s_nmax, 1)

            def probabilities(h):
                n = soft.index(h)
                dve.wait_ge(s_exp, n + 1)
                if n >= 2:
                    dve.wait_ge(s_probT, n - 1)
                src = logit[h % 2]
                if all_heads[h][0] == DIL:
                    d = dilated.index(h)
                    for m in range(MT):
                        last = dve.tensor_tensor_reduce(
                            out=prob[h % 2][:, keys(m)], in0=src[:, keys(m)], in1=counts[:, keys(m)],
                            scale=1.0, scalar=0.0, op0=ALU.mult, op1=ALU.add, accum_out=den[:, h % 2, m:m + 1])
                    last.then_inc(s_den, 1)
                    dve.wait_ge(s_den, d + 1)
                    src = prob[h % 2]
                dve.reciprocal(rden[:], den[:, h % 2, :]).then_inc(s_rden, 1)
                dve.wait_ge(s_rden, n + 1)
                for m in range(MT):
                    last = dve.tensor_scalar(prob[h % 2][:, keys(m)], src[:, keys(m)], rden[:, m:m + 1], None, ALU.mult)
                last.then_inc(s_prob, 1)

            def softplus(h):
                n = stick.index(h)
                dve.wait_ge(s_stick, 3 * n + 3)
                if n < 2:
                    dve.wait_ge(s_probT, 16)
                else:
                    dve.wait_ge(s_later, n - 1)
                dve.scalar_tensor_tensor(out=prob[h % 2][:], in0=stick_bank(h)[:, 0:SC], scalar=0.0,
                                         in1=logit[h % 2][:], op0=ALU.max, op1=ALU.add).then_inc(s_keep, 1)

            def output_low(h):
                kind, _, _, _, blk, part, _ = all_heads[h]
                rows = slice(part, part + (DS if kind == DSA else DH))
                dve.wait_ge(s_ohi, h + 1)
                dve.tensor_tensor(HTl[rows, blk, :], ps_out[rows, 0:SEQ], HTh[rows, blk, :].bitcast(F32),
                                  ALU.subtract).then_inc(s_olo, 1)

            for layer in range(DEPTH):
                st = 2 * layer
                enter(st)
                n_in = plans[layer][1]
                for slot, (_, _, _, width, _, _, _) in enumerate(plans[layer][0]):
                    if slot >= TPC:
                        low(T0[st] + slot, slot, width)
                    if slot in takes[layer]:
                        take(layer, *takes[layer][slot])
                    if layer == 0 and slot - 4 in dots_after:
                        score_terms(dots_after[slot - 4])
                    if layer == 0 and slot in topk_at:
                        topk_round(topk_at[slot])
                    if layer == 0 and slot == max(topk_at) + 1:
                        selection()
                    for h in range(H0[layer], H0[layer] + len(heads[layer])):
                        start = all_heads[h][6]
                        if slot == start + 4 and all_heads[h][0] != SB:
                            logits_max(h)
                        elif slot == start + 5 and all_heads[h][0] == SB:
                            softplus(h)
                        elif slot == start + 5:
                            probabilities(h)
                        elif slot == start + 9:
                            output_low(h)
                    for c in range(3):
                        if slot == ends[layer][n_in + c] + 4:
                            add(st, V0[st] + c, c, T0[st] + ends[layer][n_in + c] + 1)
                        if slot == ends[layer][n_in + c] + 5:
                            statistics(V0[st] + c, c)
                mlp = st + 1
                enter(mlp)

                def quarter(q):
                    for c in range(8):
                        for t in range(TPC):
                            if c or not isinstance(q, int):
                                low(q * (8 * TPC) + (T0[mlp] + c * TPC + t), t)
                            if 1 <= c <= 4 and t in (6, 7):
                                pair = 2 * (c - 1) + t - 6
                                turn_low(None, q * 8 + (hi_count(mlp) + 8 + pair), (ps_turn, ps_out)[t - 6],
                                         HTh, HTl, pair)
                            if (c >= 5 or (c == 0 and not isinstance(q, int))) and t in (3, 4):
                                n = q * 4 + (V0[mlp] + (c - 5 if c else -1))
                                if t == 3:
                                    add(mlp, n, (c - 5) % 8 % 4 if c else 3, q * (8 * TPC) + (T0[mlp] + c * TPC))
                                else:
                                    statistics(n, c - 5 if c else 3)

                quarter(0)
                with dve.Fori(1, 4) as q:
                    quarter(q)
            add(3, V0[4] - 1, 3, T0[4])
            statistics(V0[4] - 1, 3)
            aggregate(3, V0[4])
            for b in range(4):
                gained(3, b)

        @block.tensor
        def _(pe):
            pe.wait_ge(s_const_in, 48)
            pe.wait_ge(s_one, 1)
            pe.wait_ge(s_const, 8)
            pe.matmul(ps_dots[0:16, 0:OFF], table[:], bucket_sb[:, 0, :], start=True, stop=True)
            pe.matmul(ps_probT[0:16, 0:OFF], table[:], bucket_sb[:, 1, :], start=True, stop=True).then_inc(s_rows, 1)

            def multiply(tile, j, acc, hi, lo, t, first, last, width=NC):
                pe.wait_ge(s_lo, tile + 1)
                for g in range(G):
                    k = G * t + g
                    for m in range(MT):
                        dst = acc[:, m, 0:width]
                        wh, wl = whi[j % SPL][:, g, 0:width], wlo[j % SPL][:, g, 0:width]
                        xh, xl = hi[:, k, m * P:(m + 1) * P], lo[:, k, m * P:(m + 1) * P]
                        pe.matmul(dst, xl, wh, start=first and g == 0, stop=False)
                        pe.matmul(dst, xh, wl, start=False, stop=False)
                        mm = pe.matmul(dst, xh, wh, start=False, stop=last and g == G - 1)
                mm.then_inc(s_mm, 1)

            def turn_pair(turn, bank, src, pair, lag=0):
                if not (isinstance(turn, int) and turn - lag < 1):
                    pe.wait_ge(s_turned, turn - lag)
                for b in range(2):
                    for m in range(MT):
                        col = (2 * pair + b) * P
                        last = pe.transpose(bank[:, (b * MT + m) * P:(b * MT + m + 1) * P], src[:, m, col:col + P],
                                            ident[:])
                last.then_inc(s_turn, 1)

            def turn_block(stage, b):
                if stage:
                    pe.wait_ge(s_shifted, 4 * (stage - 1) + b + 1)
                elif b == 0:
                    pe.wait_ge(s_x, 16 * MT)
                for pair in (2 * b, 2 * b + 1):
                    turn_pair(U0[stage] + pair, (ps_turn, ps_out)[pair % 2], X, pair, lag=0 if pair == 0 else 1)

            def enter(stage, what=None):
                turn_block(stage, 0)
                if stage:
                    pe.wait_ge(s_added, V0[stage] - 1)
                for t in range(TPC):
                    pe.wait_ge(s_turned, U0[stage] + t + 1)
                    multiply(T0[stage] + t, t, ps[0], XTh, XTl, t, t == 0, t == TPC - 1)
                    if t in (0, 2, 4):
                        turn_block(stage, t // 2 + 1)

            def free(layer, chunk):
                what = next(w for w, c, *_ in plans[layer][0] if c == chunk)
                if what == "ki":
                    pe.wait_ge(s_ki2, 3)
                elif what == "v":
                    pe.wait_ge(s_v, v_no[layer][chunk] + 1)
                elif what == "out":
                    pe.wait_ge(s_added, V0[2 * layer] + chunk - plans[layer][1] + 1)
                else:
                    pe.wait_ge(s_stage, stage_no[layer][chunk] + 1)

            def turn_chunk(layer, what, chunk, pair):
                turn = turn_no[layer][(chunk, pair)]
                if what == "ki":
                    pe.wait_ge(s_ki2, 2)
                    pe.wait_ge(s_turned, turn)
                    for m in range(MT):
                        last = pe.transpose(ps_turn[:, m * P:(m + 1) * P], ki2[:, m, :], ident[:])
                    last.then_inc(s_turn, 1)
                    return
                pe.wait_ge(s_stage, stage_no[layer][chunk] + 1)
                turn_pair(turn, ps_turn, stage, pair)

            def dots(u):
                m, hs = dots_tile[u], dots_heads[u]
                width = P * (m + 1)
                pe.wait_ge(s_turned, turn_ki + 1)
                pe.wait_ge(s_rows_sb, 2) if u == 0 else pe.wait_ge(s_relu, u)
                for i, h in enumerate(hs):
                    rows = slice((h % 2) * DS, (h % 2 + 1) * DS)
                    last = pe.matmul(ps_dots[:, i * width:(i + 1) * width], qiT[rows, h // 2, m * P:(m + 1) * P],
                                     kiT[rows, 0:width], start=i == 0, stop=i == len(hs) - 1, skip_group_check=True)
                last.then_inc(s_dots, 1)

            def head_scores(layer, h):
                kind, parity, i, _, _, _, _ = all_heads[h]
                g = group_head(layer, h - H0[layer])
                pe.wait_ge(s_turned, turn_no[layer][(chunk_of(layer, g, "k"), 1)] + 1)
                if kind == SB:
                    n = stick.index(h)
                    if n == 0:
                        pe.wait_ge(s_nmax, 16)
                    pe.wait_ge(s_right, h - 1)
                    pe.wait_ge(s_constr, 2)
                    bank = stick_bank(h)
                    q, k = qT[parity][:, i, :], kT[parity][:, i, :]
                    pe.matmul(bank[:, 0:SEQ], k[:, 0:P], q, start=True, stop=False, skip_group_check=True)
                    pe.matmul(bank[:, SEQ:SC], k[:, P:SEQ], q[:, P:SEQ], start=False, stop=False, skip_group_check=True)
                    pe.matmul(bank[:, 0:P], neg_identr[:], not_before_r[:], start=False, stop=False, skip_group_check=True)
                    pe.matmul(bank[:, SEQ:SC], neg_identr[:], not_before_r[:], start=False, stop=True,
                              skip_group_check=True).then_inc(s_logits, 1)
                    return
                n = soft.index(h)
                if h == 0:
                    pe.wait_ge(s_relu, 6)
                elif h == H0[1]:
                    pe.wait_ge(s_right, h)
                else:
                    pe.wait_ge(s_nmax, n)
                if kind == DSA:
                    rows, blk = slice((i % 2) * DS, (i % 2 + 1) * DS), i // 2
                    pe.wait_ge(s_pick, 1)
                    pe.wait_ge(s_constr, 2)
                    pe.matmul(ps_dots[:, 0:SC], neg_identr[:], unpicked[:], start=True, stop=False,
                              skip_group_check=True)
                else:
                    rows, blk = slice(0, P), i
                q, k = qT[parity][rows, blk, :], kT[parity][rows, blk, :]
                for m in range(MT):
                    last = pe.matmul(ps_dots[:, keys(m)], q[:, m * P:(m + 1) * P], k[:, 0:P * (m + 1)],
                                     start=kind == DIL and m == 0, stop=m == 1, skip_group_check=True)
                last.then_inc(s_logits, 1)

            def head_turn(h):
                pe.wait_ge(s_prob, soft.index(h) + 1)
                if h:
                    pe.wait_ge(s_right, h)
                p = prob[h % 2]
                pe.transpose(ps_probT[:, 0:P], p[:, 0:P], ident[:])
                pe.transpose(ps_probT[:, P:SEQ], p[:, P:SEQ], ident[:])
                pe.transpose(ps_probT[:, SEQ:SC], p[:, SEQ:SC], ident[:]).then_inc(s_probT, 1)

            def stick_sum(h):
                pe.wait_ge(s_keep, stick.index(h) + 1)
                bank, sp_ = stick_bank(h), prob[h % 2]
                pe.matmul(bank[:, 0:SEQ], neg_suffix[:], sp_[:, 0:SEQ], start=False, stop=False, skip_group_check=True)
                pe.matmul(bank[:, P:SEQ], neg_ones[:], sp_[:, SEQ:SC], start=False, stop=False, skip_group_check=True)
                pe.matmul(bank[:, SEQ:SC], neg_suffix[:], sp_[:, SEQ:SC], start=False, stop=True,
                          skip_group_check=True).then_inc(s_later, 1)

            def head_output(layer, h):
                kind, parity, i, _, _, part, _ = all_heads[h]
                g = group_head(layer, h - H0[layer])
                width = DS if kind == DSA else DH
                pe.wait_ge(s_v, v_no[layer][chunk_of(layer, g, "v")] + 1)
                pe.wait_ge(s_right, h + 1)
                if h:
                    pe.wait_ge(s_olo, h)
                cols = slice(i * width, (i + 1) * width)
                dst = ps_out[part:part + width, :]
                pe.matmul(dst[:, 0:SEQ], v[parity][:, 0, cols], probT[:, 0:SEQ], start=True, stop=False)
                pe.matmul(dst[:, P:SEQ], v[parity][:, 1, cols], probT[:, SEQ:SC], start=False,
                          stop=True).then_inc(s_pv, 1)

            for layer in range(DEPTH):
                st = 2 * layer
                enter(st)
                plan, n_in = plans[layer]
                for slot, (what, chunk, _, width, t, first, last) in enumerate(plan):
                    if slot >= TPC:
                        if first:
                            if chunk >= 2:
                                free(layer, chunk - 2)
                            elif st:
                                pe.wait_ge(s_added, V0[st])
                        if what == "out":
                            done = max(h for h in range(H0[layer], H0[layer] + len(heads[layer]))
                                       if all_heads[h][4] // G == t)
                            pe.wait_ge(s_olo, done + 1)
                            multiply(T0[st] + slot, slot, ps[chunk % 2], HTh, HTl, t, first, last, width)
                        else:
                            multiply(T0[st] + slot, slot, ps[chunk % 2], XTh, XTl, t, first, last, width)
                    if slot in turns[layer]:
                        turn_chunk(layer, *turns[layer][slot])
                    if layer == 0 and slot in dots_after:
                        dots(dots_after[slot])
                    for h in range(H0[layer], H0[layer] + len(heads[layer])):
                        start = all_heads[h][6]
                        if slot == start:
                            head_scores(layer, h)
                        elif slot == start + 3 and all_heads[h][0] == SB:
                            stick_sum(h)
                        elif slot == start + 3:
                            head_turn(h)
                        elif slot == start + 5:
                            head_output(layer, h)
                mlp = st + 1
                enter(mlp)

                def quarter(q):
                    for c in range(8):
                        if c == 1 or (c == 0 and not isinstance(q, int)):
                            pe.wait_ge(s_added, q * 4 + (V0[mlp] - 1 + c))
                        elif 2 <= c <= 5:
                            pe.wait_ge(s_stage, q * 4 + (B0[mlp] + c - 1))
                        elif c >= 6:
                            pe.wait_ge(s_added, q * 4 + (V0[mlp] + c - 5))
                        hi, lo = (XTh, XTl) if c < 4 else (HTh, HTl)
                        for t in range(TPC):
                            if c == 4:
                                pe.wait_ge(s_turned, q * 8 + (U0[mlp] + 8 + t + 1))
                            if c or not isinstance(q, int):
                                multiply(q * (8 * TPC) + (T0[mlp] + c * TPC + t), t, ps[c % 2], hi, lo, t,
                                         t == 0, t == TPC - 1)
                            if 1 <= c <= 4 and t in (2, 3):
                                if t == 2:
                                    pe.wait_ge(s_square, q * 4 + (16 * layer + c))
                                turn_pair(q * 8 + (U0[mlp] + 8 + 2 * (c - 1) + t - 2), (ps_turn, ps_out)[t - 2], squared,
                                          t - 2, lag=1)

                quarter(0)
                with pe.Fori(1, 4) as q:
                    quarter(q)


_INS = ["x", "even_w_in", "even_w_out", "odd_w_in", "odd_w_out", "rel_bias", "ln_mix_g", "ln_mix_b",
        "ffn_w1", "ffn_w2", "ln_ffn_g", "ln_ffn_b"]


def shape_constants():
    dist = SEQ - 1 - np.arange(OFF)
    back = np.maximum(dist, 0)
    exact = N_BUCKETS // 2
    large = exact + (np.log(np.maximum(back, 1).astype(np.float32) / np.float32(exact))
                     / np.float32(np.log(BUCKET_MAX_DIST / exact)) * np.float32(N_BUCKETS - exact)).astype(np.int32)
    bucket = np.where(back < exact, back, np.minimum(large, N_BUCKETS - 1))
    reach = np.zeros(OFF, np.float32)
    for window, dilation in CONFIGS:
        reach += (dist >= 0) & (dist % dilation == 0) & (dist // dilation <= window // dilation)
    rows = np.zeros((N_BUCKETS + 1, 2, OFF), np.float32)
    rows[bucket, :, np.arange(OFF)] = 1.0
    rows[N_BUCKETS, 0] = np.where(dist >= 0, 0.0, NEG)
    rows[N_BUCKETS, 1] = np.where(reach > 0, 0.0, NEG)
    t, s = np.arange(P)[:, None], np.arange(SEQ)[None, :]
    count = np.concatenate([reach[SEQ - 1 - (t - s[:, :P])], reach[SEQ - 1 - (t + P - s)]], axis=1)
    return {"bucket_rows": rows, "branch_count": count}


def kernel(**inputs):
    import concourse.bacc as _bacc
    from concourse.bass_utils import run_bass_kernel_spmd as _run

    nc = _bacc.Bacc("TRN2", target_bir_lowering=False, num_devices=1)
    arrays, args = {}, []
    for name, a in [(n, inputs[n]) for n in _INS] + list(shape_constants().items()):
        a = np.ascontiguousarray(a)
        arrays[f"in_{name}_dram"] = a
        args.append(nc.dram_tensor(f"in_{name}_dram", a.shape, mybir.dt.from_np(a.dtype), kind="ExternalInput").ap())
    args.append(nc.dram_tensor("out_0_dram", (1, SEQ, D), F32, kind="ExternalOutput").ap())
    hybrid_trunk(nc, *args)
    r = _run(nc, [arrays], core_ids=[0])
    return r.results[0]["out_0_dram"]
```

```python
from contextlib import ExitStack

import concourse.bass as bass
import numpy as np
from concourse import mybir

ALU = mybir.AluOpType
ACT = mybir.ActivationFunctionType
F32 = mybir.dt.float32
F32R = mybir.dt.float32r

P = 128
SEQ = 256
D = 2048
MT = SEQ // P
KB = D // P
NC = 512
G = 2
TPC = KB // G
RAW = 4
SPL = 8
HALF = D // 2
DH = 128
DS = 64
N_IDX = 8
TOPK = min(256, SEQ // 4)
D_FF = 4 * D
DEPTH = 2
ALPHA = (2 * DEPTH) ** 0.25
LN_EPS = 1e-5
NEG = -1e30
LOWEST = -3e38
N_BUCKETS = 32
BUCKET_MAX_DIST = 2048
CONFIGS = ((128, 1), (512, 4), (2048, 16))
SC = P + SEQ
OFF = 2 * SEQ - 1

SB, DSA, DIL = "stick-breaking", "sparse", "dilated"


def head_schedule(even):
    heads = []
    if even:
        for g in range(2):
            k_end = 16 + 24 * g + 15
            for i in range(8):
                n = 8 * g + i
                heads.append((DSA, g % 2, i, n, HALF // P + n // 2, (n % 2) * DS, k_end + 6 + 3 * i))
        for g in range(2, 4):
            k_end = 16 + 24 * g + 15
            for i in range(4):
                heads.append((SB, g % 2, i, None, 4 * (g - 2) + i, 0, k_end + 6 + (3 if g == 3 else 6) * i))
    else:
        for g in range(4):
            k_end = 24 * g + 15
            for i in range(4):
                n = 4 * g + i
                heads.append((DIL, g % 2, i, n, n, 0, k_end + 6 + (2 if g == 3 else 6) * i))
    return heads


def mixer_plan(even):
    chunks = []
    if even:
        chunks += [("qi", 6 * HALF, NC), ("ki", 6 * HALF + N_IDX * DS, DS + N_IDX)]
        starts = [(3 * HALF, c) for c in range(2)] + [(0, c) for c in range(2)]
        for base, c in starts:
            chunks += [(n, base + i * HALF + c * NC, NC) for i, n in enumerate("qkv")]
        late = [0, 1, 4, 5, 6, 7, 2, 3]
    else:
        for c in range(4):
            chunks += [(n, i * D + c * NC, NC) for i, n in enumerate("qkv")]
        late = list(range(8))
    slots = [
        (what, n, col, width, t, t == 0, t == TPC - 1)
        for n, (what, col, width) in enumerate(chunks)
        for t in range(TPC)
    ]
    n_in = len(chunks)
    order = [(0, t) for t in range(6)] + [(1, t) for t in range(6)]
    order += [(0, 6), (0, 7), (1, 6), (1, 7)] + [(c, t) for c in (2, 3) for t in range(8)]
    slots += [("out", n_in + c, c * NC, NC, late[t], t == 0, t == TPC - 1) for c, t in order]
    return slots, n_in


def hybrid_trunk(nc, x, even_w_in, even_w_out, odd_w_in, odd_w_out, rel_bias,
                 ln_mix_g, ln_mix_b, ffn_w1, ffn_w2, ln_ffn_g, ln_ffn_b,
                 bucket_rows, branch_count, out):
    with ExitStack() as ctx:
        top = [(nc.sbuf_base + 63) // 64 * 64]

        def sb(name, shape, dt=F32, at=None):
            offset = top[0] if at is None else at
            size = 4 * int(np.prod(shape[1:]))
            if at is None:
                top[0] = offset + (size + 63) // 64 * 64
            return nc.alloc_sbuf_tensor_at(name, shape, dt, offset=offset)

        def sem(name):
            return ctx.enter_context(nc.semaphore(name))

        X = sb("X", [P, MT, D])
        XTh, XTl = sb("XTh", [P, KB, SEQ], F32R), sb("XTl", [P, KB, SEQ], F32R)
        HTh, HTl = sb("HTh", [P, KB, SEQ], F32R), sb("HTl", [P, KB, SEQ], F32R)
        raw = [sb(f"raw{i}", [P, G, NC]) for i in range(RAW)]
        whi = [sb(f"whi{i}", [P, G, NC], F32R) for i in range(SPL)]
        wlo = [sb(f"wlo{i}", [P, G, NC], F32R) for i in range(SPL)]
        group_at = top[0]
        qT, kT, v = [], [], []
        for i in range(2):
            qT.append(sb(f"qT{i}", [P, 4, SEQ]))
            kT.append(sb(f"kT{i}", [P, 4, SEQ]))
            v.append(sb(f"v{i}", [P, MT, NC]))
        gain = sb("gain", [P, D], at=group_at)
        shift = sb("shift", [P, D], at=group_at + 4 * D)
        bucket_sb = sb("bucket_sb", [N_BUCKETS + 1, 2, OFF], at=group_at)
        bias_rows = sb("bias_rows", [16, 2, OFF + 1], at=group_at + 8 * 4 * SEQ)
        index_at = [group_at + 12 * 4 * SEQ]

        def sb_index(name, shape):
            at = index_at[0]
            index_at[0] += (4 * int(np.prod(shape[1:])) + 63) // 64 * 64
            assert index_at[0] <= group_at + 24 * 4 * SEQ
            return sb(name, shape, at=at)

        qiT = sb_index("qiT", [P, 4, SEQ])
        kiT = sb_index("kiT", [P, SEQ])
        ki2 = sb_index("ki2", [P, MT, 2 * DS])
        relu_dots = sb_index("relu_dots", [P, NC])
        score = sb_index("score", [P, SC])
        work = sb_index("work", [P, SC])
        wi = sb("wi", [P, MT, N_IDX])
        top8 = sb("top8", [P, MT, 8])
        unpicked = sb("unpicked", [P, SC], F32R)
        stage = sb("stage", [P, MT, NC])
        squared = sb("squared", [P, MT, NC], at=top[0])
        logit = [sb(f"logit{i}", [P, SC]) for i in range(2)]
        prob = [sb(f"prob{i}", [P, SC]) for i in range(2)]
        bias = [sb(f"bias{i}", [P, SC]) for i in range(2)]
        probT = sb("probT", [P, SC])
        row_max = sb("row_max", [P, MT])
        neg_max = sb("neg_max", [P, MT])
        den = sb("den", [P, 2, MT])
        rden = sb("rden", [P, MT])
        stats = sb("stats", [P, MT, 4, 6])
        mean_var = sb("mean_var", [P, MT, 2])
        var_eps = sb("var_eps", [P, MT])
        minus_half = sb("minus_half", [P, MT])
        rstd = sb("rstd", [P, MT])
        shift_mean = sb("shift_mean", [P, MT])
        ident = sb("ident", [P, P])
        neg_identr = sb("neg_identr", [P, P], F32R)
        not_before = sb("not_before", [P, P])
        not_before_r = sb("not_before_r", [P, P], F32R)
        neg_suffix = sb("neg_suffix", [P, P])
        neg_ones = sb("neg_ones", [P, P])
        counts = sb("counts", [P, SC])
        table = sb("table", [N_BUCKETS + 1, 16])
        assert top[0] <= nc.sbuf_usable_end, top[0]
        rows_dram = nc.dram_tensor("bias_rows_dram", [16, 2, P, OFF + 1], F32, kind="Internal")

        ps = [ctx.enter_context(nc.psum_tensor(f"ps{i}", [P, MT, NC], F32)) for i in range(2)]
        ps_dots = ctx.enter_context(nc.psum_tensor("ps_dots", [P, NC], F32))
        ps_probT = ctx.enter_context(nc.psum_tensor("ps_probT", [P, NC], F32))
        ps_turn = ctx.enter_context(nc.psum_tensor("ps_turn", [P, NC], F32))
        ps_out = ctx.enter_context(nc.psum_tensor("ps_out", [P, NC], F32))

        s_x = [sem(f"x_loaded{b}") for b in range(4)]
        s_const_in = sem("constants_loaded")
        s_one = sem("ones_row_built")
        s_const = sem("constants_built")
        s_constr = sem("constants_rounded")
        s_rows = sem("bias_rows_computed")
        s_rows_sb = sem("bias_rows_copied")
        s_rows_dram = sem("bias_rows_in_dram")
        s_raw = [sem(f"raw_loaded{i}") for i in range(RAW)]
        s_hi = sem("weights_high")
        s_lo = sem("weights_low")
        s_mm = sem("tile_multiplied")
        s_stage = sem("chunk_staged")
        s_square = sem("chunk_squared")
        s_v = sem("v_ready")
        s_ki2 = sem("indexer_key_staged")
        s_half = sem("first_tokens_multiplied")
        s_last = sem("last_chunk_added")
        s_added = sem("chunk_added")
        s_stat = sem("chunk_statistics")
        s_turn = sem("blocks_transposed")
        s_turn_hi = sem("blocks_high")
        s_turned = sem("blocks_taken")
        s_gain = sem("gain_loaded")
        s_aggr = sem("mean_variance")
        s_var = sem("variance_guarded")
        s_rstd = sem("rstd_ready")
        s_centre = sem("centre_ready")
        s_centred = sem("block_centred")
        s_gained = sem("block_gained")
        s_shifted = sem("block_shifted")
        s_alpha = sem("residual_scaled")
        s_dots = sem("indexer_dots")
        s_relu = sem("indexer_relu")
        s_score = sem("score_terms")
        s_causal = sem("score_masked")
        s_top = sem("topk_steps")
        s_pick = sem("selection_ready")
        s_bias = [sem(f"bias_loaded{i}") for i in range(2)]
        s_logits = sem("head_dots")
        s_max = sem("row_max_ready")
        s_nmax = sem("neg_max_ready")
        s_exp = sem("exponentials")
        s_den = sem("denominator_ready")
        s_rden = sem("reciprocal_ready")
        s_prob = sem("probabilities")
        s_probT = sem("prob_transposed")
        s_stick = sem("stick_steps")
        s_keep = sem("stick_softplus")
        s_later = sem("stick_cumsum")
        s_right = sem("right_operand")
        s_pv = sem("head_output")
        s_ohi = sem("head_output_high")
        s_olo = sem("head_output_low")
        s_tail = sem("block_shifted_by_dve")
        s_store = sem("output_stored")

        plans = [mixer_plan(True), mixer_plan(False)]
        heads = [head_schedule(True), head_schedule(False)]
        H0 = [0, len(heads[0])]
        T0, V0, U0, B0 = [0], [0], [0], [0]
        for layer in range(DEPTH):
            plan, n_in = plans[layer]
            staged = sum(last and what in ("qi", "q", "k") for what, _, _, _, _, _, last in plan)
            mixer = (len(plan), 3, 8 + 2 * staged + (layer == 0), staged)
            mlp = (32 * TPC, 15, 8 + 32, 16)
            for tiles, adds, pairs, stages in (mixer, mlp):
                T0.append(T0[-1] + tiles)
                V0.append(V0[-1] + adds)
                U0.append(U0[-1] + pairs)
                B0.append(B0[-1] + stages)
        N_T = T0[-1]
        all_heads = heads[0] + heads[1]
        soft = [h for h, head in enumerate(all_heads) if head[0] != SB]
        stick = [h for h, head in enumerate(all_heads) if head[0] == SB]
        dilated = [h for h, head in enumerate(all_heads) if head[0] == DIL]

        turns, takes, leaves, ends = [{}, {}], [{}, {}], [{}, {}], [{}, {}]
        turn_no, stage_no, v_no, stage_free = [{}, {}], [{}, {}], [{}, {}], [{}, {}]
        for layer in range(DEPTH):
            turn, staged, free = U0[2 * layer] + 8, B0[2 * layer], None
            for slot, (what, chunk, _, _, _, _, last) in enumerate(plans[layer][0]):
                if last:
                    ends[layer][chunk] = slot
                if not last or what == "out":
                    continue
                leaves[layer][slot + 4] = (what, chunk)
                if what == "v":
                    v_no[layer][chunk] = sum(map(len, v_no))
                    continue
                for pair in range(1 if what == "ki" else 2):
                    turns[layer][slot + 2 + 2 * pair] = (what, chunk, pair)
                    takes[layer][slot + 6 + 2 * pair] = (what, chunk, pair)
                    turn_no[layer][(chunk, pair)] = turn
                    turn += 1
                if what != "ki":
                    stage_no[layer][chunk] = staged
                    stage_free[layer][chunk] = free
                    free = turn
                    staged += 1
        turn_ki = turn_no[0][(1, 0)]
        idx_lead = 2
        dots_after = {19 + u: u for u in range(6)}
        dots_heads = [(0, 2, 4, 6), (1, 3, 5, 7), (0, 2), (4, 6), (1, 3), (5, 7)]
        dots_tile = [0, 0, 1, 1, 1, 1]
        topk_at = {29 + r: r for r in range(TOPK // 8)}

        def group_of(layer, chunk):
            return (chunk - (idx_lead if layer == 0 else 0)) // 3

        def chunk_of(layer, group, what):
            return 3 * group + "qkv".index(what) + (idx_lead if layer == 0 else 0)

        def heads_before(layer, group):
            per = [8, 8, 4, 4] if layer == 0 else [4] * 4
            return H0[layer] + sum(per[:group + 1])

        def group_head(layer, n):
            per = [8, 8, 4, 4] if layer == 0 else [4] * 4
            return next(g for g in range(4) if n < sum(per[:g + 1]))

        def keys(m):
            return slice(0, P) if m == 0 else slice(P, SC)

        def stick_bank(h):
            return (ps_dots, ps_probT)[stick.index(h) % 2]

        def mlp_tile(mlp, q, c, t):
            return q * (8 * TPC) + (T0[mlp] + (4 + c) * TPC + t)

        def units_before(b):
            return 2 * b + 2

        block = ctx.enter_context(nc.Block())

        @block.sync
        def _(sp):
            rows = x[0].rearrange("(m p) d -> p m d", p=P)

            def load_x(b):
                cols = slice(b * NC, (b + 1) * NC)
                sp.dma_start(X[:, :, cols], rows[:, :, cols]).then_inc(s_x[b], 16)

            load_x(0)

            def load(w, tile, j, row, col, width=NC):
                if not (isinstance(tile, int) and tile < RAW):
                    sp.wait_ge(s_lo, tile - RAW + 1)
                src = w[bass.ds(row, G * P), bass.ds(col, width)].rearrange("(g p) n -> p g n", p=P)
                sp.dma_start(raw[j % RAW][:, :, 0:width], src).then_inc(s_raw[j % RAW], 16)

            for layer in range(DEPTH):
                w_in = even_w_in[0] if layer == 0 else odd_w_in[0]
                w_out = even_w_out[0] if layer == 0 else odd_w_out[0]
                for slot, (what, chunk, col, width, t, _, _) in enumerate(plans[layer][0]):
                    load(w_out if what == "out" else w_in, T0[2 * layer] + slot, slot, t * G * P, col, width)
                    if layer == 0 and slot < 3:
                        load_x(slot + 1)

                def chunks(q, cs):
                    for c in cs:
                        for t in range(TPC):
                            tile = mlp_tile(2 * layer + 1, q, c, t)
                            if c < 4:
                                load(ffn_w2[layer], tile, t, q * D + t * G * P, c * NC)
                            else:
                                load(ffn_w1[layer], tile, t, t * G * P, q * D + (D + (c - 4) * NC))

                chunks(-1, range(4, 8))
                with sp.Fori(0, 3) as q:
                    chunks(q, range(8))
                chunks(3, range(4))
            rows_out = out[0].rearrange("(m p) d -> p m d", p=P)
            for m in range(MT):
                for b in range(4):
                    if m == 1 and b % 2 == 0:
                        sp.wait_ge(s_tail, b // 2 + 1)
                    elif m == 1:
                        sp.wait_ge(s_shifted, 8 * 3 + 4 + b // 2 + 1)
                    else:
                        sp.wait_ge(s_shifted, 8 * 3 + b + 1)
                    cols = slice(b * NC, (b + 1) * NC)
                    sp.dma_start(rows_out[:, m, cols], X[:, m, cols]).then_inc(s_store, 16)
            sp.wait_ge(s_store, 8 * 16)

        @block.gpsimd
        def _(pool):
            pool.dma_start(bucket_sb[:], bucket_rows).then_inc(s_const_in, 16)
            pool.dma_start(table[0:N_BUCKETS, :], rel_bias).then_inc(s_const_in, 16)
            pool.dma_start(counts[:], branch_count).then_inc(s_const_in, 16)
            pool.memset(ident[:], 0.0).then_inc(s_const, 1)
            pool.memset(not_before[:], 0.0).then_inc(s_const, 1)
            pool.memset(neg_suffix[:], -1.0).then_inc(s_const, 1)
            pool.memset(neg_ones[:], -1.0).then_inc(s_const, 1)
            pool.memset(minus_half[:], -0.5).then_inc(s_const, 1)
            pool.wait_ge(s_const, 5)
            pool.affine_select(out=ident[:], in_=ident[:], compare_op=ALU.not_equal, fill=1.0, base=0,
                               pattern=[[-1, P]], channel_multiplier=1).then_inc(s_const, 1)
            pool.affine_select(out=not_before[:], in_=not_before[:], compare_op=ALU.is_gt, fill=1.0, base=0,
                               pattern=[[1, P]], channel_multiplier=-1).then_inc(s_const, 1)
            pool.affine_select(out=neg_suffix[:], in_=neg_suffix[:], compare_op=ALU.is_ge, fill=0.0, base=0,
                               pattern=[[-1, P]], channel_multiplier=1).then_inc(s_const, 1)
            pool.wait_ge(s_rows_sb, 2)
            for k in range(2):
                copies = bass.AP(bias_rows, k * (OFF + 1), [[2 * (OFF + 1), 16], [0, P], [1, OFF]])
                pool.dma_start(rows_dram.ap()[:, k, :, 0:OFF], copies).then_inc(s_rows_dram, 16)
            pool.wait_ge(s_rows_dram, 32)

            def load_bias(h):
                kind, _, _, row, _, _, _ = all_heads[h]
                n = soft.index(h)
                if n >= 2:
                    pool.wait_ge(s_nmax, n - 1)
                start = (row * 2 + (kind == DIL)) * P * (OFF + 1) + SEQ - 1
                rows = rows_dram.ap()
                pool.dma_start(bias[n % 2][:, keys(0)], bass.AP(rows.tensor, start, [[OFF, P], [1, P]]))\
                    .then_inc(s_bias[n % 2], 16)
                pool.dma_start(bias[n % 2][:, keys(1)], bass.AP(rows.tensor, start - P, [[OFF, P], [1, SEQ]]))\
                    .then_inc(s_bias[n % 2], 16)

            def scale_residual(st):
                for m in range(MT):
                    for b in range(4):
                        pool.wait_ge(s_turn, U0[st] + (4 * m + b if st else 2 * b + m) + 1)
                        xb = X[:, m, b * NC:(b + 1) * NC]
                        pool.tensor_scalar(xb, xb, ALPHA, None, ALU.mult).then_inc(s_alpha, 1)

            def norm(n, gains, shifts):
                pool.dma_start(gain[:], bass.AP(gains.tensor, gains.offset, [[0, P], [1, D]])).then_inc(s_gain, 16)
                pool.dma_start(shift[:], bass.AP(shifts.tensor, shifts.offset, [[0, P], [1, D]])).then_inc(s_gain, 16)
                for m in range(MT):
                    pool.wait_ge(s_aggr, 2 * n + m + 1)
                    pool.tensor_scalar(var_eps[:, m:m + 1], mean_var[:, m, 1:2], LN_EPS, None, ALU.add)\
                        .then_inc(s_var, 1)
                    pool.wait_ge(s_var, 2 * n + m + 1)
                    pool.tensor_tensor(rstd[:, m:m + 1], var_eps[:, m:m + 1], minus_half[:, 0:1], ALU.pow)\
                        .then_inc(s_rstd, 1)
                    if m == 0:
                        pool.wait_ge(s_gain, 32 * (n + 1))
                    for b in range(4):
                        if n == 3 and m == 1 and b % 2 == 0:
                            continue
                        pool.wait_ge(s_gained, 8 * n + 4 * m + b + 1)
                        xb = X[:, m, b * NC:(b + 1) * NC]
                        pool.tensor_tensor(xb, xb, shift[:, b * NC:(b + 1) * NC], ALU.add).then_inc(s_shifted, 1)

            for layer in range(DEPTH):
                scale_residual(2 * layer)
                own = [h for h in soft if H0[layer] <= h < H0[layer] + len(heads[layer])]
                for h in own[:2]:
                    load_bias(h)
                if layer == 0:
                    for m in range(MT):
                        pool.wait_ge(s_score, N_IDX * (m + 1))
                        pool.affine_select(out=score[:, keys(m)], in_=score[:, keys(m)], compare_op=ALU.is_ge,
                                           fill=NEG, base=m * P, pattern=[[-1, P * (m + 1)]],
                                           channel_multiplier=1).then_inc(s_causal, 1)
                for h in own[2:]:
                    load_bias(h)
                pool.wait_ge(s_pv, H0[layer] + len(heads[layer]))
                norm(2 * layer, ln_mix_g[layer], ln_mix_b[layer])
                scale_residual(2 * layer + 1)
                mlp = 2 * layer + 1

                with pool.Fori(0, 4) as q:
                    for c in range(4):
                        pool.wait_ge(s_stage, q * 4 + (B0[mlp] + c + 1))
                        pool.wait_ge(s_turn, q * 8 + (U0[mlp] + 8 + 2 * c))
                        pool.tensor_tensor(squared[:], stage[:], stage[:], ALU.mult).then_inc(s_square, 1)
                norm(mlp, ln_ffn_g[layer], ln_ffn_b[layer])

        @block.scalar
        def _(act):
            def high(tile, lap, j, width=NC):
                act.wait_ge(s_raw[j % RAW], lap)
                if not (isinstance(tile, int) and tile < SPL):
                    act.wait_ge(s_mm, tile - SPL + 1)
                act.activation(whi[j % SPL][:, :, 0:width], raw[j % RAW][:, :, 0:width], ACT.Copy).then_inc(s_hi, 1)

            def high_at(tile, width=NC):
                high(tile, 16 * (tile // RAW + 1), tile, width)

            def turn_high(turn, bank, dst, pair):
                act.wait_ge(s_turn, turn + 1)
                act.activation(dst[:, 2 * pair:2 * pair + 2, :], bank[:].rearrange("p (b t) -> p b t", b=2),
                               ACT.Copy).then_inc(s_turn_hi, 1)

            def turn_high_x(turn, m, b):
                act.wait_ge(s_turn, turn + 1)
                act.activation(XTh[:, 4 * b:4 * b + 4, m * P:(m + 1) * P],
                               (ps_turn, ps_out)[turn % 2][:].rearrange("p (b t) -> p b t", b=4),
                               ACT.Copy).then_inc(s_turn_hi, 1)

            def centre(n, m, b):
                if b == 0:
                    act.wait_ge(s_centre, 2 * n + m + 1)
                xb = X[:, m, b * NC:(b + 1) * NC]
                act.activation(xb, xb, ACT.Identity, bias=shift_mean[:, m:m + 1],
                               scale=rstd[:, m:m + 1]).then_inc(s_centred, 1)

            def start():
                for t in range(TPC):
                    if t % 2 == 0:
                        for m in range(MT):
                            turn_high_x(t + m, m, t // 2)
                    high_at(t)

            def cross(n):
                tl, tf, u0 = T0[n + 1] - TPC, T0[n + 1], U0[n + 1]
                for t in range(TPC):
                    high_at(tl + t)
                if n == 3:
                    for m in range(MT):
                        for b in range(4):
                            centre(n, m, b)
                    return
                high_at(tf)
                centre(n, 0, 0)
                centre(n, 0, 1)
                high_at(tf + 1)
                high_at(tf + 2)
                centre(n, 0, 2)
                centre(n, 0, 3)
                high_at(tf + 3)
                high_at(tf + 4)
                turn_high_x(u0, 0, 0)
                high_at(tf + 5)
                high_at(tf + 6)
                turn_high_x(u0 + 1, 0, 1)
                high_at(tf + 7)
                turn_high_x(u0 + 2, 0, 2)
                centre(n, 1, 0)
                centre(n, 1, 1)
                turn_high_x(u0 + 3, 0, 3)
                centre(n, 1, 2)
                centre(n, 1, 3)
                for b in range(4):
                    turn_high_x(u0 + 4 + b, 1, b)

            def leave(layer, what, chunk):
                act.wait_ge(s_mm, T0[2 * layer] + ends[layer][chunk] + 1)
                acc = ps[chunk % 2]
                if what == "ki":
                    for i in range(2):
                        act.activation(ki2[:, :, i * DS:(i + 1) * DS], acc[:, :, 0:DS], ACT.Copy).then_inc(s_ki2, 1)
                    act.activation(wi[:], acc[:, :, DS:DS + N_IDX], ACT.Copy, scale=N_IDX ** -0.5).then_inc(s_ki2, 1)
                elif what == "v":
                    g = group_of(layer, chunk)
                    if g >= 2:
                        act.wait_ge(s_pv, heads_before(layer, g - 2))
                    if layer == 0 and g == 0:
                        act.wait_ge(s_rows_dram, 32)
                    act.activation(v[g % 2][:], acc[:], ACT.Copy).then_inc(s_v, 1)
                else:
                    sparse = what == "qi" or (layer == 0 and group_of(layer, chunk) < 2)
                    scale = 1.0 if what == "k" else (DS if sparse else DH) ** -0.5
                    if stage_free[layer][chunk] is not None:
                        act.wait_ge(s_turn, stage_free[layer][chunk])
                    act.activation(stage[:], acc[:], ACT.Copy, scale=scale).then_inc(s_stage, 1)

            def relu_dots_of(u):
                act.wait_ge(s_dots, u + 1)
                if u:
                    act.wait_ge(s_score, (0, 4, 8, 10, 12, 14)[u])
                act.activation(relu_dots[:], ps_dots[:], ACT.Relu).then_inc(s_relu, 1)

            def exponentials(h):
                act.wait_ge(s_nmax, soft.index(h) + 1)
                for m in range(MT):
                    lg = logit[h % 2][:, keys(m)]
                    if all_heads[h][0] == DSA:
                        last = act.activation(lg, lg, ACT.Exp, bias=neg_max[:, m:m + 1],
                                              accum_out=den[:, h % 2, m:m + 1])
                    else:
                        last = act.activation(lg, lg, ACT.Exp, bias=neg_max[:, m:m + 1])
                last.then_inc(s_exp, 1)

            def stick_log(h):
                n = stick.index(h)
                act.wait_ge(s_logits, h + 1)
                act.wait_ge(s_right, h - 1)
                act.activation(logit[h % 2][:], stick_bank(h)[:, 0:SC], ACT.Abs).then_inc(s_stick, 1)
                act.wait_ge(s_stick, 3 * n + 1)
                act.activation(logit[h % 2][:], logit[h % 2][:], ACT.Exp, scale=-1.0).then_inc(s_stick, 1)
                act.wait_ge(s_stick, 3 * n + 2)
                act.activation(logit[h % 2][:], logit[h % 2][:], ACT.Ln, bias=1.0).then_inc(s_stick, 1)

            def right_operand(h):
                if h:
                    act.wait_ge(s_pv, h)
                if all_heads[h][0] == SB:
                    act.wait_ge(s_later, stick.index(h) + 1)
                    act.activation(probT[:], stick_bank(h)[:, 0:SC], ACT.Exp).then_inc(s_right, 1)
                else:
                    act.wait_ge(s_probT, soft.index(h) + 1)
                    act.activation(probT[:], ps_probT[:, 0:SC], ACT.Copy).then_inc(s_right, 1)

            def output_high(h):
                kind, _, _, _, blk, part, _ = all_heads[h]
                rows = slice(part, part + (DS if kind == DSA else DH))
                act.wait_ge(s_pv, h + 1)
                act.activation(HTh[rows, blk, :], ps_out[rows, 0:SEQ], ACT.Copy).then_inc(s_ohi, 1)

            start()
            act.wait_ge(s_const, 8)
            act.activation(neg_identr[:], ident[:], ACT.Copy, scale=NEG).then_inc(s_constr, 1)
            act.activation(not_before_r[:], not_before[:], ACT.Copy).then_inc(s_constr, 1)
            act.wait_ge(s_rows, 1)
            act.activation(bias_rows[:, 0, 0:OFF], ps_dots[0:16, 0:OFF], ACT.Copy).then_inc(s_rows_sb, 1)
            act.activation(bias_rows[:, 1, 0:OFF], ps_probT[0:16, 0:OFF], ACT.Copy).then_inc(s_rows_sb, 1)
            for layer in range(DEPTH):
                t0 = T0[2 * layer]
                plan = plans[layer][0]
                for slot in range(TPC, len(plan) - TPC):
                    high_at(t0 + slot, plan[slot][3])
                    if slot in leaves[layer]:
                        leave(layer, *leaves[layer][slot])
                    if layer == 0 and slot - 4 in dots_after:
                        relu_dots_of(dots_after[slot - 4])
                    for h in range(H0[layer], H0[layer] + len(heads[layer])):
                        begin = all_heads[h][6]
                        if slot == begin + 4 and all_heads[h][0] == SB:
                            stick_log(h)
                        elif slot == begin + 4:
                            exponentials(h)
                        elif slot == begin + 7:
                            right_operand(h)
                        elif slot == begin + 9:
                            output_high(h)
                mlp = 2 * layer + 1
                cross(2 * layer)

                def chunks(q, cs):
                    for c in cs:
                        relu = 4 * q + (3 if c == 0 else c - 1)
                        for t in range(TPC):
                            tile = mlp_tile(mlp, q, c, t)
                            high(tile, q * (8 * TPC * 16 // RAW) + 16 * ((mlp_tile(mlp, 0, c, t)) // RAW + 1), t)
                            if 1 <= c <= 4:
                                continue
                            if t == 3:
                                act.wait_ge(s_mm, mlp_tile(mlp, q, c, 0))
                                if not (isinstance(relu, int) and 16 * layer + relu == 0):
                                    act.wait_ge(s_square, relu + 16 * layer)
                                act.activation(stage[:], ps[(c - 1) % 2][:], ACT.Relu).then_inc(s_stage, 1)
                            if t in (6, 7):
                                pair = (6 if c == 0 else 2 * (c - 5)) + t - 6
                                turn = (8 * q if c == 0 else 8 * q + 8) + (U0[mlp] + 8 + pair)
                                turn_high(turn, (ps_turn, ps_out)[t - 6], HTh, pair)

                chunks(-1, range(5, 8))
                with act.Fori(0, 3) as q:
                    chunks(q, range(8))
                chunks(3, range(3))
                cross(mlp)

        @block.vector
        def _(dve):
            dve.memset(table[N_BUCKETS:N_BUCKETS + 1, :], 1.0).then_inc(s_one, 1)

            def low(tile, j, width=NC):
                dve.wait_ge(s_hi, tile + 1)
                if not (isinstance(tile, int) and tile < SPL):
                    dve.wait_ge(s_mm, tile - SPL + 1)
                dve.tensor_tensor(wlo[j % SPL][:, :, 0:width], raw[j % RAW][:, :, 0:width],
                                  whi[j % SPL][:, :, 0:width].bitcast(F32), ALU.subtract).then_inc(s_lo, 1)

            def turn_low(turn_hi, bank, hi, lo, pair):
                dve.wait_ge(s_turn_hi, turn_hi + 1)
                dve.tensor_tensor(lo[:, 2 * pair:2 * pair + 2, :], bank[:].rearrange("p (b t) -> p b t", b=2),
                                  hi[:, 2 * pair:2 * pair + 2, :].bitcast(F32), ALU.subtract).then_inc(s_turned, 1)

            def turn_low_x(turn, turn_hi, m, b):
                dve.wait_ge(s_turn_hi, turn_hi + 1)
                part = (slice(None), slice(4 * b, 4 * b + 4), slice(m * P, (m + 1) * P))
                dve.tensor_tensor(XTl[part], (ps_turn, ps_out)[turn % 2][:].rearrange("p (b t) -> p b t", b=4),
                                  XTh[part].bitcast(F32), ALU.subtract).then_inc(s_turned, 1)

            def add(st, c, done):
                dve.wait_ge(s_mm, done)
                dve.wait_ge(s_alpha, 8 * st + 8)
                xb = X[:, :, c * NC:(c + 1) * NC]
                dve.tensor_tensor(xb, ps[c % 2][:], xb, ALU.add).then_inc(s_added, 1)

            def statistics(n, c):
                dve.wait_ge(s_added, n + 1)
                for m in range(MT):
                    last = dve.bn_stats(stats[:, m, c, :], X[:, m, c * NC:(c + 1) * NC])
                last.then_inc(s_stat, 1)

            def last_chunk(n, m):
                if m == 0:
                    dve.wait_ge(s_half, n + 1)
                else:
                    dve.wait_ge(s_mm, T0[n + 1])
                xb = X[:, m, 3 * NC:D]
                dve.tensor_tensor(xb, ps[1][:, m, :], xb, ALU.add).then_inc(s_last, 1)
                dve.wait_ge(s_last, 2 * n + m + 1)
                dve.bn_stats(stats[:, m, 3, :], xb).then_inc(s_stat, 1)
                dve.wait_ge(s_stat, V0[n + 1] + 2 * n + m + 1)
                dve.bn_aggr(mean_var[:, m, :], stats[:, m, :, :]).then_inc(s_aggr, 1)

            def centring(n, m):
                dve.wait_ge(s_rstd, 2 * n + m + 1)
                dve.scalar_tensor_tensor(out=shift_mean[:, m:m + 1], in0=mean_var[:, m, 0:1], scalar=-1.0,
                                         in1=rstd[:, m:m + 1], op0=ALU.mult, op1=ALU.mult).then_inc(s_centre, 1)

            def gained(n, m, b):
                dve.wait_ge(s_centred, 8 * n + 4 * m + b + 1)
                if m == b == 0:
                    dve.wait_ge(s_gain, 32 * (n + 1))
                xb = X[:, m, b * NC:(b + 1) * NC]
                dve.tensor_tensor(xb, xb, gain[:, b * NC:(b + 1) * NC], ALU.mult).then_inc(s_gained, 1)

            def hi_count(st):
                return sum((8, 40)[i % 2] for i in range(st))

            def start():
                for t in range(TPC):
                    if t % 2 == 0:
                        for m in range(MT):
                            turn_low_x(t + m, t + m, m, t // 2)
                    low(t, t)

            def cross(n):
                tl, tf, u0, h0 = T0[n + 1] - TPC, T0[n + 1], U0[n + 1], hi_count(n + 1)
                for t in range(TPC):
                    low(tl + t, t)
                    if t == 3:
                        add(n, 2, tl)
                    if t == 4:
                        statistics(V0[n + 1] - 1, 2)
                last_chunk(n, 0)
                if n == 3:
                    centring(n, 0)
                    for b in range(4):
                        gained(n, 0, b)
                    last_chunk(n, 1)
                    centring(n, 1)
                    for b in range(4):
                        gained(n, 1, b)
                        if b % 2 == 0:
                            dve.wait_ge(s_gained, 8 * n + 4 + b + 1)
                            xb = X[:, 1, b * NC:(b + 1) * NC]
                            dve.tensor_tensor(xb, xb, shift[:, b * NC:(b + 1) * NC], ALU.add).then_inc(s_tail, 1)
                    return
                low(tf, 0)
                centring(n, 0)
                low(tf + 1, 1)
                gained(n, 0, 0)
                gained(n, 0, 1)
                low(tf + 2, 2)
                gained(n, 0, 2)
                gained(n, 0, 3)
                low(tf + 3, 3)
                low(tf + 4, 4)
                turn_low_x(u0, h0, 0, 0)
                low(tf + 5, 5)
                low(tf + 6, 6)
                last_chunk(n, 1)
                turn_low_x(u0 + 1, h0 + 1, 0, 1)
                low(tf + 7, 7)
                centring(n, 1)
                turn_low_x(u0 + 2, h0 + 2, 0, 2)
                gained(n, 1, 0)
                gained(n, 1, 1)
                turn_low_x(u0 + 3, h0 + 3, 0, 3)
                gained(n, 1, 2)
                gained(n, 1, 3)
                for b in range(4):
                    turn_low_x(u0 + 4 + b, h0 + 4 + b, 1, b)

            def take(layer, what, chunk, pair):
                turn = turn_no[layer][(chunk, pair)]
                dve.wait_ge(s_turn, turn + 1)
                if what == "q" and layer == 0:
                    dve.wait_ge(s_rows, 1)
                if what == "ki":
                    dve.tensor_copy(kiT[:], ps_turn[:, 0:SEQ]).then_inc(s_turned, 1)
                    return
                if what == "qi":
                    dst = qiT
                else:
                    g = group_of(layer, chunk)
                    dst = (qT if what == "q" else kT)[g % 2]
                    if g >= 2:
                        dve.wait_ge(s_logits, heads_before(layer, g - 2))
                dve.tensor_copy(dst[:, 2 * pair:2 * pair + 2, :],
                                ps_turn[:].rearrange("p (b t) -> p b t", b=2)).then_inc(s_turned, 1)

            def score_terms(u):
                m, hs = dots_tile[u], dots_heads[u]
                dve.wait_ge(s_relu, u + 1)
                dve.wait_ge(s_ki2, 3)
                width = P * (m + 1)
                for i, h in enumerate(hs):
                    n = (0, 4, 8, 10, 12, 14)[u] + i
                    term = relu_dots[:, i * width:(i + 1) * width]
                    if n % N_IDX == 0:
                        dve.tensor_scalar(score[:, keys(m)], term, wi[:, m, h:h + 1], None, ALU.mult).then_inc(s_score, 1)
                        continue
                    dve.wait_ge(s_score, n)
                    dve.scalar_tensor_tensor(out=score[:, keys(m)], in0=term, scalar=wi[:, m, h:h + 1],
                                             in1=score[:, keys(m)], op0=ALU.mult, op1=ALU.add).then_inc(s_score, 1)

            def topk_round(r):
                src = score if r == 0 else work
                if r == 0:
                    dve.wait_ge(s_causal, MT)
                else:
                    dve.wait_ge(s_top, 4 * r)
                for m in range(MT):
                    dve.max(top8[:, m, :], src[:, keys(m)]).then_inc(s_top, 1)
                for m in range(MT):
                    dve.wait_ge(s_top, 4 * r + m + 1)
                    dve.match_replace(work[:, keys(m)], top8[:, m, :], src[:, keys(m)], LOWEST).then_inc(s_top, 1)

            def selection():
                dve.wait_ge(s_top, 4 * (TOPK // 8))
                dve.tensor_tensor(unpicked[:], work[:], score[:], ALU.is_equal).then_inc(s_pick, 1)

            def logits_max(h):
                n = soft.index(h)
                dve.wait_ge(s_logits, h + 1)
                dve.wait_ge(s_bias[n % 2], 32 * (n // 2 + 1))
                if h >= 2:
                    dve.wait_ge(s_right, h - 1)
                for m in range(MT):
                    last = dve.tensor_tensor_reduce(
                        out=logit[h % 2][:, keys(m)], in0=ps_dots[:, keys(m)], in1=bias[n % 2][:, keys(m)],
                        scale=1.0, scalar=LOWEST, op0=ALU.add, op1=ALU.max, accum_out=row_max[:, m:m + 1])
                last.then_inc(s_max, 1)
                dve.wait_ge(s_max, n + 1)
                if n:
                    dve.wait_ge(s_exp, n)
                dve.tensor_scalar(neg_max[:], row_max[:], -1.0, None, ALU.mult).then_inc(s_nmax, 1)

            def probabilities(h):
                n = soft.index(h)
                dve.wait_ge(s_exp, n + 1)
                if n >= 2:
                    dve.wait_ge(s_probT, n - 1)
                src = logit[h % 2]
                if all_heads[h][0] == DIL:
                    d = dilated.index(h)
                    for m in range(MT):
                        last = dve.tensor_tensor_reduce(
                            out=prob[h % 2][:, keys(m)], in0=src[:, keys(m)], in1=counts[:, keys(m)],
                            scale=1.0, scalar=0.0, op0=ALU.mult, op1=ALU.add, accum_out=den[:, h % 2, m:m + 1])
                    last.then_inc(s_den, 1)
                    dve.wait_ge(s_den, d + 1)
                    src = prob[h % 2]
                dve.reciprocal(rden[:], den[:, h % 2, :]).then_inc(s_rden, 1)
                dve.wait_ge(s_rden, n + 1)
                for m in range(MT):
                    last = dve.tensor_scalar(prob[h % 2][:, keys(m)], src[:, keys(m)], rden[:, m:m + 1], None, ALU.mult)
                last.then_inc(s_prob, 1)

            def softplus(h):
                n = stick.index(h)
                dve.wait_ge(s_stick, 3 * n + 3)
                if n < 2:
                    dve.wait_ge(s_probT, 16)
                else:
                    dve.wait_ge(s_later, n - 1)
                dve.scalar_tensor_tensor(out=prob[h % 2][:], in0=stick_bank(h)[:, 0:SC], scalar=0.0,
                                         in1=logit[h % 2][:], op0=ALU.max, op1=ALU.add).then_inc(s_keep, 1)

            def output_low(h):
                kind, _, _, _, blk, part, _ = all_heads[h]
                rows = slice(part, part + (DS if kind == DSA else DH))
                dve.wait_ge(s_ohi, h + 1)
                dve.tensor_tensor(HTl[rows, blk, :], ps_out[rows, 0:SEQ], HTh[rows, blk, :].bitcast(F32),
                                  ALU.subtract).then_inc(s_olo, 1)

            start()
            for layer in range(DEPTH):
                st = 2 * layer
                plan, n_in = plans[layer]
                for slot in range(TPC, len(plan) - TPC):
                    low(T0[st] + slot, slot, plan[slot][3])
                    if slot in takes[layer]:
                        take(layer, *takes[layer][slot])
                    if layer == 0 and slot - 4 in dots_after:
                        score_terms(dots_after[slot - 4])
                    if layer == 0 and slot in topk_at:
                        topk_round(topk_at[slot])
                    if layer == 0 and slot == max(topk_at) + 1:
                        selection()
                    for h in range(H0[layer], H0[layer] + len(heads[layer])):
                        begin = all_heads[h][6]
                        if slot == begin + 4 and all_heads[h][0] != SB:
                            logits_max(h)
                        elif slot == begin + 5 and all_heads[h][0] == SB:
                            softplus(h)
                        elif slot == begin + 5:
                            probabilities(h)
                        elif slot == begin + 9:
                            output_low(h)
                    for c in range(2):
                        if slot == ends[layer][n_in + c] + 4:
                            add(st, c, T0[st] + ends[layer][n_in + c] + 1)
                        if slot == ends[layer][n_in + c] + 5:
                            statistics(V0[st] + c, c)
                mlp = st + 1
                cross(st)

                def chunks(q, cs):
                    for c in cs:
                        for t in range(TPC):
                            low(mlp_tile(mlp, q, c, t), t)
                            if not 1 <= c <= 4 and t in (6, 7):
                                pair = (6 if c == 0 else 2 * (c - 5)) + t - 6
                                taken = (8 * q if c == 0 else 8 * q + 8) + (hi_count(mlp) + 8 + pair)
                                turn_low(taken, (ps_turn, ps_out)[t - 6], HTh, HTl, pair)
                            if 1 <= c <= 4 and t == 3:
                                add(mlp, c - 1, mlp_tile(mlp, q, c, 0))
                            if 1 <= c <= 4 and t == 4:
                                statistics(q * 4 + (V0[mlp] + c - 1), c - 1)

                chunks(-1, range(5, 8))
                with dve.Fori(0, 3) as q:
                    chunks(q, range(8))
                chunks(3, range(3))
                cross(mlp)

        @block.tensor
        def _(pe):
            def multiply(tile, j, acc, hi, lo, t, first, last, width=NC, tokens=range(MT), half=False):
                pe.wait_ge(s_lo, tile + 1)
                for g in range(G):
                    k = G * t + g
                    for m in tokens:
                        dst = acc[:, m, 0:width]
                        wh, wl = whi[j % SPL][:, g, 0:width], wlo[j % SPL][:, g, 0:width]
                        xh, xl = hi[:, k, m * P:(m + 1) * P], lo[:, k, m * P:(m + 1) * P]
                        pe.matmul(dst, xl, wh, start=first and g == 0, stop=False)
                        pe.matmul(dst, xh, wl, start=False, stop=False)
                        mm = pe.matmul(dst, xh, wh, start=False, stop=last and g == G - 1)
                if MT - 1 in tokens:
                    mm.then_inc(s_mm, 1)
                elif last and half:
                    mm.then_inc(s_half, 1)

            def turn_pair(turn, bank, src, pair, lag=0):
                if not (isinstance(turn, int) and turn - lag < 1):
                    pe.wait_ge(s_turned, turn - lag)
                for b in range(2):
                    for m in range(MT):
                        col = (2 * pair + b) * P
                        last = pe.transpose(bank[:, (b * MT + m) * P:(b * MT + m + 1) * P], src[:, m, col:col + P],
                                            ident[:])
                last.then_inc(s_turn, 1)

            def turn_x(turn, m, b, first=False):
                if turn:
                    pe.wait_ge(s_turned, turn if first else turn - 1)
                bank = (ps_turn, ps_out)[turn % 2]
                for k in range(4):
                    last = pe.transpose(bank[:, k * P:(k + 1) * P], X[:, m, (4 * b + k) * P:(4 * b + k + 1) * P],
                                        ident[:])
                last.then_inc(s_turn, 1)

            def start():
                pe.wait_ge(s_const, 6)
                for t in range(TPC):
                    if t % 2 == 0:
                        pe.wait_ge(s_x[t // 2], 16)
                        for m in range(MT):
                            turn_x(t + m, m, t // 2)
                        pe.wait_ge(s_turned, t + 2)
                    multiply(t, t, ps[0], XTh, XTl, t, t == 0, t == TPC - 1)
                pe.wait_ge(s_const_in, 48)
                pe.wait_ge(s_const, 8)
                pe.wait_ge(s_one, 1)
                pe.matmul(ps_dots[0:16, 0:OFF], table[:], bucket_sb[:, 0, :], start=True, stop=True)
                pe.matmul(ps_probT[0:16, 0:OFF], table[:], bucket_sb[:, 1, :], start=True,
                          stop=True).then_inc(s_rows, 1)

            def cross(n, t_of_slot):
                tl, tf, u0 = T0[n + 1] - TPC, T0[n + 1], U0[n + 1]

                def normed(m, b, first=False):
                    pe.wait_ge(s_shifted, 8 * n + 4 * m + b + 1)
                    turn_x(u0 + 4 * m + b, m, b, first)

                for i, t in enumerate(t_of_slot):
                    multiply(tl + i, i, ps[1], HTh, HTl, t, i == 0, i == TPC - 1, tokens=(0,),
                             half=True)
                for i, t in enumerate(t_of_slot):
                    multiply(tl + i, i, ps[1], HTh, HTl, t, i == 0, i == TPC - 1, tokens=(1,))
                    if n < 3 and i == 5:
                        normed(0, 0, first=True)
                    if n < 3 and i == 7:
                        normed(0, 1)
                if n == 3:
                    return
                pe.wait_ge(s_added, V0[n + 1])
                for m in range(MT):
                    for t in range(TPC):
                        pe.wait_ge(s_turned, u0 + 4 * m + t // 2 + 1)
                        multiply(tf + t, t, ps[0], XTh, XTl, t, t == 0, t == TPC - 1, tokens=(m,))
                        if t in (1, 3):
                            normed(m, 2 + t // 2)
                        if m == 0 and t in (5, 7):
                            normed(1, (t - 5) // 2)

            def free(layer, chunk):
                what = next(w for w, c, *_ in plans[layer][0] if c == chunk)
                if what == "ki":
                    pe.wait_ge(s_ki2, 3)
                elif what == "v":
                    pe.wait_ge(s_v, v_no[layer][chunk] + 1)
                elif what == "out":
                    pe.wait_ge(s_added, V0[2 * layer] + chunk - plans[layer][1] + 1)
                else:
                    pe.wait_ge(s_stage, stage_no[layer][chunk] + 1)

            def turn_chunk(layer, what, chunk, pair):
                turn = turn_no[layer][(chunk, pair)]
                if what == "ki":
                    pe.wait_ge(s_ki2, 2)
                    pe.wait_ge(s_turned, turn)
                    for m in range(MT):
                        last = pe.transpose(ps_turn[:, m * P:(m + 1) * P], ki2[:, m, :], ident[:])
                    last.then_inc(s_turn, 1)
                    return
                pe.wait_ge(s_stage, stage_no[layer][chunk] + 1)
                turn_pair(turn, ps_turn, stage, pair)

            def dots(u):
                m, hs = dots_tile[u], dots_heads[u]
                width = P * (m + 1)
                pe.wait_ge(s_turned, turn_ki + 1)
                pe.wait_ge(s_rows_sb, 2) if u == 0 else pe.wait_ge(s_relu, u)
                for i, h in enumerate(hs):
                    rows = slice((h % 2) * DS, (h % 2 + 1) * DS)
                    last = pe.matmul(ps_dots[:, i * width:(i + 1) * width], qiT[rows, h // 2, m * P:(m + 1) * P],
                                     kiT[rows, 0:width], start=i == 0, stop=i == len(hs) - 1, skip_group_check=True)
                last.then_inc(s_dots, 1)

            def head_scores(layer, h):
                kind, parity, i, _, _, _, _ = all_heads[h]
                g = group_head(layer, h - H0[layer])
                pe.wait_ge(s_turned, turn_no[layer][(chunk_of(layer, g, "k"), 1)] + 1)
                if kind == SB:
                    n = stick.index(h)
                    if n == 0:
                        pe.wait_ge(s_nmax, 16)
                    pe.wait_ge(s_right, h - 1)
                    pe.wait_ge(s_constr, 2)
                    bank = stick_bank(h)
                    q, k = qT[parity][:, i, :], kT[parity][:, i, :]
                    pe.matmul(bank[:, 0:SEQ], k[:, 0:P], q, start=True, stop=False, skip_group_check=True)
                    pe.matmul(bank[:, SEQ:SC], k[:, P:SEQ], q[:, P:SEQ], start=False, stop=False, skip_group_check=True)
                    pe.matmul(bank[:, 0:P], neg_identr[:], not_before_r[:], start=False, stop=False, skip_group_check=True)
                    pe.matmul(bank[:, SEQ:SC], neg_identr[:], not_before_r[:], start=False, stop=True,
                              skip_group_check=True).then_inc(s_logits, 1)
                    return
                n = soft.index(h)
                if h == 0:
                    pe.wait_ge(s_relu, 6)
                elif h == H0[1]:
                    pe.wait_ge(s_right, h)
                else:
                    pe.wait_ge(s_nmax, n)
                if kind == DSA:
                    rows, blk = slice((i % 2) * DS, (i % 2 + 1) * DS), i // 2
                    pe.wait_ge(s_pick, 1)
                    pe.wait_ge(s_constr, 2)
                    pe.matmul(ps_dots[:, 0:SC], neg_identr[:], unpicked[:], start=True, stop=False,
                              skip_group_check=True)
                else:
                    rows, blk = slice(0, P), i
                q, k = qT[parity][rows, blk, :], kT[parity][rows, blk, :]
                for m in range(MT):
                    last = pe.matmul(ps_dots[:, keys(m)], q[:, m * P:(m + 1) * P], k[:, 0:P * (m + 1)],
                                     start=kind == DIL and m == 0, stop=m == 1, skip_group_check=True)
                last.then_inc(s_logits, 1)

            def head_turn(h):
                pe.wait_ge(s_prob, soft.index(h) + 1)
                if h:
                    pe.wait_ge(s_right, h)
                p = prob[h % 2]
                pe.transpose(ps_probT[:, 0:P], p[:, 0:P], ident[:])
                pe.transpose(ps_probT[:, P:SEQ], p[:, P:SEQ], ident[:])
                pe.transpose(ps_probT[:, SEQ:SC], p[:, SEQ:SC], ident[:]).then_inc(s_probT, 1)

            def stick_sum(h):
                pe.wait_ge(s_keep, stick.index(h) + 1)
                bank, sp_ = stick_bank(h), prob[h % 2]
                pe.matmul(bank[:, 0:SEQ], neg_suffix[:], sp_[:, 0:SEQ], start=False, stop=False, skip_group_check=True)
                pe.matmul(bank[:, P:SEQ], neg_ones[:], sp_[:, SEQ:SC], start=False, stop=False, skip_group_check=True)
                pe.matmul(bank[:, SEQ:SC], neg_suffix[:], sp_[:, SEQ:SC], start=False, stop=True,
                          skip_group_check=True).then_inc(s_later, 1)

            def head_output(layer, h):
                kind, parity, i, _, _, part, _ = all_heads[h]
                g = group_head(layer, h - H0[layer])
                width = DS if kind == DSA else DH
                pe.wait_ge(s_v, v_no[layer][chunk_of(layer, g, "v")] + 1)
                pe.wait_ge(s_right, h + 1)
                if h:
                    pe.wait_ge(s_olo, h)
                cols = slice(i * width, (i + 1) * width)
                dst = ps_out[part:part + width, :]
                pe.matmul(dst[:, 0:SEQ], v[parity][:, 0, cols], probT[:, 0:SEQ], start=True, stop=False)
                pe.matmul(dst[:, P:SEQ], v[parity][:, 1, cols], probT[:, SEQ:SC], start=False,
                          stop=True).then_inc(s_pv, 1)

            start()
            for layer in range(DEPTH):
                st = 2 * layer
                plan, n_in = plans[layer]
                for slot in range(TPC, len(plan) - TPC):
                    what, chunk, _, width, t, first, last = plan[slot]
                    if first:
                        if chunk >= 2:
                            free(layer, chunk - 2)
                        elif st:
                            pe.wait_ge(s_last, 2 * st)
                    if what == "out":
                        done = max(h for h in range(H0[layer], H0[layer] + len(heads[layer]))
                                   if all_heads[h][4] // G == t)
                        pe.wait_ge(s_olo, done + 1)
                        multiply(T0[st] + slot, slot, ps[chunk % 2], HTh, HTl, t, first, last, width)
                    else:
                        multiply(T0[st] + slot, slot, ps[chunk % 2], XTh, XTl, t, first, last, width)
                    if slot in turns[layer]:
                        turn_chunk(layer, *turns[layer][slot])
                    if layer == 0 and slot in dots_after:
                        dots(dots_after[slot])
                    for h in range(H0[layer], H0[layer] + len(heads[layer])):
                        begin = all_heads[h][6]
                        if slot == begin:
                            head_scores(layer, h)
                        elif slot == begin + 3 and all_heads[h][0] == SB:
                            stick_sum(h)
                        elif slot == begin + 3:
                            head_turn(h)
                        elif slot == begin + 5:
                            head_output(layer, h)
                mlp = st + 1
                free(layer, n_in + 1)
                cross(st, [s[4] for s in plan[-TPC:]])

                def chunks(q, cs):
                    for c in cs:
                        if c == 5 and isinstance(q, int):
                            pe.wait_ge(s_last, 2 * mlp)
                        elif c in (0, 1):
                            pe.wait_ge(s_stage, q * 4 + (B0[mlp] + c + 3))
                        elif c <= 5:
                            pe.wait_ge(s_added, q * 4 + (V0[mlp] + c - 1))
                        else:
                            pe.wait_ge(s_stage, q * 4 + (B0[mlp] + c - 1))
                        hi, lo = (HTh, HTl) if c < 4 else (XTh, XTl)
                        for t in range(TPC):
                            if c == 0:
                                pe.wait_ge(s_turned, q * 8 + (U0[mlp] + 8 + t + 1))
                            multiply(mlp_tile(mlp, q, c, t), t, ps[c % 2], hi, lo, t, t == 0, t == TPC - 1)
                            if not 1 <= c <= 4 and t in (2, 3):
                                pair = (6 if c == 0 else 2 * (c - 5)) + t - 2
                                if t == 2:
                                    pe.wait_ge(s_square, q * 4 + (16 * layer + (4 if c == 0 else c)))
                                turn_pair((8 * q if c == 0 else 8 * q + 8) + (U0[mlp] + 8 + pair),
                                          (ps_turn, ps_out)[t - 2], squared, t - 2, lag=1)

                chunks(-1, range(5, 8))
                with pe.Fori(0, 3) as q:
                    chunks(q, range(8))
                chunks(3, range(3))
                pe.wait_ge(s_added, V0[mlp] + 14)
                cross(mlp, range(TPC))


_INS = ["x", "even_w_in", "even_w_out", "odd_w_in", "odd_w_out", "rel_bias", "ln_mix_g", "ln_mix_b",
        "ffn_w1", "ffn_w2", "ln_ffn_g", "ln_ffn_b"]


def shape_constants():
    dist = SEQ - 1 - np.arange(OFF)
    back = np.maximum(dist, 0)
    exact = N_BUCKETS // 2
    large = exact + (np.log(np.maximum(back, 1).astype(np.float32) / np.float32(exact))
                     / np.float32(np.log(BUCKET_MAX_DIST / exact)) * np.float32(N_BUCKETS - exact)).astype(np.int32)
    bucket = np.where(back < exact, back, np.minimum(large, N_BUCKETS - 1))
    reach = np.zeros(OFF, np.float32)
    for window, dilation in CONFIGS:
        reach += (dist >= 0) & (dist % dilation == 0) & (dist // dilation <= window // dilation)
    rows = np.zeros((N_BUCKETS + 1, 2, OFF), np.float32)
    rows[bucket, :, np.arange(OFF)] = 1.0
    rows[N_BUCKETS, 0] = np.where(dist >= 0, 0.0, NEG)
    rows[N_BUCKETS, 1] = np.where(reach > 0, 0.0, NEG)
    t, s = np.arange(P)[:, None], np.arange(SEQ)[None, :]
    count = np.concatenate([reach[SEQ - 1 - (t - s[:, :P])], reach[SEQ - 1 - (t + P - s)]], axis=1)
    return {"bucket_rows": rows, "branch_count": count}


def kernel(**inputs):
    import concourse.bacc as _bacc
    from concourse.bass_utils import run_bass_kernel_spmd as _run

    nc = _bacc.Bacc("TRN2", target_bir_lowering=False, num_devices=1)
    arrays, args = {}, []
    for name, a in [(n, inputs[n]) for n in _INS] + list(shape_constants().items()):
        a = np.ascontiguousarray(a)
        arrays[f"in_{name}_dram"] = a
        args.append(nc.dram_tensor(f"in_{name}_dram", a.shape, mybir.dt.from_np(a.dtype), kind="ExternalInput").ap())
    args.append(nc.dram_tensor("out_0_dram", (1, SEQ, D), F32, kind="ExternalOutput").ap())
    hybrid_trunk(nc, *args)
    r = _run(nc, [arrays], core_ids=[0])
    return r.results[0]["out_0_dram"]
```

```python
from contextlib import ExitStack

import concourse.bass as bass
import numpy as np
from concourse import mybir

ALU = mybir.AluOpType
ACT = mybir.ActivationFunctionType
F32 = mybir.dt.float32
F32R = mybir.dt.float32r

P = 128
SEQ = 256
D = 2048
MT = SEQ // P
KB = D // P
NC = 512
G = 2
TPC = KB // G
RAW = 4
SPL = 8
HALF = D // 2
DH = 128
DS = 64
N_IDX = 8
TOPK = min(256, SEQ // 4)
D_FF = 4 * D
DEPTH = 2
ALPHA = (2 * DEPTH) ** 0.25
LN_EPS = 1e-5
NEG = -1e30
LOWEST = -3e38
N_BUCKETS = 32
BUCKET_MAX_DIST = 2048
CONFIGS = ((128, 1), (512, 4), (2048, 16))
SC = P + SEQ
OFF = SEQ + P - 1
KI = DS + N_IDX
KT = 2

SB, DSA, DIL = "stick-breaking", "sparse", "dilated"


def head_schedule(even):
    heads = []
    if even:
        for g in range(2):
            k_end = TPC + KT + 24 * g + 15
            for i in range(8):
                n = 8 * g + i
                heads.append((DSA, g % 2, i, n, HALF // P + n // 2, (n % 2) * DS, k_end + 6 + 3 * i))
        for g in range(2, 4):
            k_end = TPC + KT + 24 * g + 15
            for i in range(4):
                heads.append((SB, g % 2, i, None, 4 * (g - 2) + i, 0, k_end + 6 + (3 if g == 3 else 6) * i))
    else:
        for g in range(4):
            k_end = 24 * g + 15
            for i in range(4):
                n = 4 * g + i
                heads.append((DIL, g % 2, i, n, n, 0, k_end + 6 + (2 if g == 3 else 6) * i))
    return heads


def mixer_plan(even):
    chunks = []
    if even:
        chunks += [("qi", 6 * HALF, NC), ("ki", 6 * HALF + N_IDX * DS, KI)]
        starts = [(3 * HALF, c) for c in range(2)] + [(0, c) for c in range(2)]
        for base, c in starts:
            chunks += [(n, base + i * HALF + c * NC, NC) for i, n in enumerate("qkv")]
        late = [0, 1, 4, 5, 6, 7, 2, 3]
    else:
        for c in range(4):
            chunks += [(n, i * D + c * NC, NC) for i, n in enumerate("qkv")]
        late = list(range(8))
    slots = [
        (what, n, col, width, t, t == 0, last)
        for n, (what, col, width) in enumerate(chunks)
        for t in range(KT if what == "ki" else TPC)
        for last in [t == (KT if what == "ki" else TPC) - 1]
    ]
    n_in = len(chunks)
    order = [(0, t) for t in range(6)] + [(1, t) for t in range(6)]
    order += [(0, 6), (0, 7), (1, 6), (1, 7)] + [(c, t) for c in (2, 3) for t in range(8)]
    slots += [("out", n_in + c, c * NC, NC, late[t], t == 0, t == TPC - 1) for c, t in order]
    return slots, n_in


def hybrid_trunk(nc, x, even_w_in, even_w_out, odd_w_in, odd_w_out, rel_bias,
                 ln_mix_g, ln_mix_b, ffn_w1, ffn_w2, ln_ffn_g, ln_ffn_b,
                 bucket_rows, branch_count, out):
    with ExitStack() as ctx:
        top = [(nc.sbuf_base + 63) // 64 * 64]

        def sb(name, shape, dt=F32, at=None):
            offset = top[0] if at is None else at
            size = 4 * int(np.prod(shape[1:]))
            if at is None:
                top[0] = offset + (size + 63) // 64 * 64
            return nc.alloc_sbuf_tensor_at(name, shape, dt, offset=offset)

        def sem(name):
            return ctx.enter_context(nc.semaphore(name))

        X = sb("X", [P, MT, D])
        XTh, XTl = sb("XTh", [P, KB, SEQ], F32R), sb("XTl", [P, KB, SEQ], F32R)
        HTh, HTl = sb("HTh", [P, KB, SEQ], F32R), sb("HTl", [P, KB, SEQ], F32R)
        raw = [sb(f"raw{i}", [P, G, NC]) for i in range(RAW)]
        whi = [sb(f"whi{i}", [P, G, NC], F32R) for i in range(SPL)]
        wlo = [sb(f"wlo{i}", [P, G, NC], F32R) for i in range(SPL)]
        group_at = top[0]
        qT, kT, v = [], [], []
        for i in range(2):
            qT.append(sb(f"qT{i}", [P, 4, SEQ]))
            kT.append(sb(f"kT{i}", [P, 4, SEQ]))
            v.append(sb(f"v{i}", [P, MT, NC]))
        gain = sb("gain", [P, D], at=group_at)
        shift = sb("shift", [P, D], at=group_at + 4 * D)
        bucket_sb = sb("bucket_sb", [N_BUCKETS + 1, 2, OFF], at=group_at)
        bias_rows = sb("bias_rows", [16, 2, OFF], at=group_at + 8 * 4 * SEQ)
        index_at = [group_at + 12 * 4 * SEQ]

        def sb_index(name, shape):
            at = index_at[0]
            index_at[0] += (4 * int(np.prod(shape[1:])) + 63) // 64 * 64
            assert index_at[0] <= group_at + 24 * 4 * SEQ
            return sb(name, shape, at=at)

        qiT = sb_index("qiT", [P, 4, SEQ])
        kiT = sb_index("kiT", [P, SEQ])
        wiT = sb_index("wiT", [P, SEQ])
        relu_dots = sb_index("relu_dots", [P, NC])
        score = sb_index("score", [P, SC])
        work = sb_index("work", [P, SC])
        wi = sb("wi", [P, MT, N_IDX])
        top8 = sb("top8", [P, MT, 8])
        unpicked = sb("unpicked", [P, SC])
        stage = sb("stage", [P, MT, NC])
        squared = sb("squared", [P, MT, NC], at=top[0])
        logit = [sb(f"logit{i}", [P, SC]) for i in range(2)]
        prob = [sb(f"prob{i}", [P, SC]) for i in range(2)]
        bias = [sb(f"bias{i}", [P, SEQ]) for i in range(2)]
        probT = sb("probT", [P, SC])
        row_max = sb("row_max", [P, MT])
        neg_max = sb("neg_max", [P, MT])
        den = sb("den", [P, 2, MT])
        rden = sb("rden", [P, MT])
        stats = sb("stats", [P, MT, 4, 6])
        mean_var = sb("mean_var", [P, MT, 2])
        var_eps = sb("var_eps", [P, MT])
        minus_half = sb("minus_half", [P, MT])
        rstd = sb("rstd", [P, MT])
        ident = sb("ident", [P, P])
        neg_identr = sb("neg_identr", [P, P], F32R)
        not_before = sb("not_before", [P, P])
        not_before_r = sb("not_before_r", [P, 2, P], F32R)
        neg_suffix = sb("neg_suffix", [P, P])
        neg_ones = sb("neg_ones", [P, P])
        counts = sb("counts", [P, SEQ])
        table = sb("table", [N_BUCKETS + 1, 16])
        assert top[0] <= nc.sbuf_usable_end, top[0]
        rows_dram = nc.dram_tensor("bias_rows_dram", [16, 2, OFF], F32, kind="Internal")
        copies_dram = nc.dram_tensor("bias_copies_dram", [16, 2, P, OFF + 1], F32, kind="Internal")

        ps = [ctx.enter_context(nc.psum_tensor(f"ps{i}", [P, MT, NC], F32)) for i in range(2)]
        ps_dots = ctx.enter_context(nc.psum_tensor("ps_dots", [P, NC], F32))
        ps_probT = ctx.enter_context(nc.psum_tensor("ps_probT", [P, NC], F32))
        ps_turn = ctx.enter_context(nc.psum_tensor("ps_turn", [P, NC], F32))
        ps_out = ctx.enter_context(nc.psum_tensor("ps_out", [P, NC], F32))

        s_x = [[sem(f"x_loaded{m}_{b}") for b in range(4)] for m in range(MT)]
        s_const_in = sem("constants_loaded")
        s_one = sem("ones_row_built")
        s_const = sem("constants_built")
        s_constr = sem("constants_rounded")
        s_rows = sem("bias_rows_computed")
        s_rows_sb = sem("bias_rows_copied")
        s_rows_dram = sem("bias_rows_in_dram")
        s_copies = [sem(f"bias_row_copied_for_tokens{i}") for i in range(4)]
        s_raw = [sem(f"raw_loaded{i}") for i in range(RAW)]
        s_hi = sem("weights_high")
        s_lo = sem("weights_low")
        s_mm = sem("tile_multiplied")
        s_stage = sem("chunk_staged")
        s_square = sem("chunk_squared")
        s_v = sem("v_ready")
        s_ki = sem("indexer_key_staged")
        s_ki_copy = sem("indexer_key_doubled")
        s_half = sem("first_tokens_multiplied")
        s_last = sem("last_chunk_added")
        s_added = sem("chunk_added")
        s_stat = sem("chunk_statistics")
        s_turn = sem("blocks_transposed")
        s_turn_hi = sem("blocks_high")
        s_turned = sem("blocks_taken")
        s_gain = sem("gain_loaded")
        s_aggr = sem("mean_variance")
        s_var = sem("variance_guarded")
        s_rstd = sem("rstd_ready")
        s_gained = sem("block_gained")
        s_scaled = sem("block_scaled")
        s_shifted = sem("block_shifted")
        s_alpha = sem("residual_scaled")
        s_dots = sem("indexer_dots")
        s_relu = sem("indexer_relu")
        s_score = sem("score_terms")
        s_causal = sem("score_masked")
        s_top = sem("topk_steps")
        s_pick = sem("selection_ready")
        s_bias = [sem(f"bias_loaded{i}") for i in range(2)]
        s_masked = sem("bias_masked")
        s_logits = sem("head_dots")
        s_max = sem("row_max_ready")
        s_nmax = sem("neg_max_ready")
        s_exp = sem("exponentials")
        s_den = sem("denominator_ready")
        s_rden = sem("reciprocal_ready")
        s_prob = sem("probabilities")
        s_probT = sem("prob_transposed")
        s_stick = sem("stick_steps")
        s_keep = sem("stick_softplus")
        s_later = sem("stick_cumsum")
        s_right = sem("right_operand")
        s_pv = sem("head_output")
        s_ohi = sem("head_output_high")
        s_olo = sem("head_output_low")
        s_tail = sem("block_shifted_by_dve")
        s_store = sem("output_stored")

        plans = [mixer_plan(True), mixer_plan(False)]
        heads = [head_schedule(True), head_schedule(False)]
        H0 = [0, len(heads[0])]
        T0, V0, U0, B0 = [0], [0], [0], [0]
        for layer in range(DEPTH):
            plan, n_in = plans[layer]
            staged = sum(last and what in ("qi", "q", "k") for what, _, _, _, _, _, last in plan)
            mixer = (len(plan), 3, 8 + 2 * staged + (layer == 0), staged)
            mlp = (32 * TPC, 15, 8 + 32, 16)
            for tiles, adds, pairs, stages in (mixer, mlp):
                T0.append(T0[-1] + tiles)
                V0.append(V0[-1] + adds)
                U0.append(U0[-1] + pairs)
                B0.append(B0[-1] + stages)
        N_T = T0[-1]
        all_heads = heads[0] + heads[1]
        soft = [h for h, head in enumerate(all_heads) if head[0] != SB]
        stick = [h for h, head in enumerate(all_heads) if head[0] == SB]
        dilated = [h for h, head in enumerate(all_heads) if head[0] == DIL]

        turns, takes, leaves, ends = [{}, {}], [{}, {}], [{}, {}], [{}, {}]
        turn_no, stage_no, v_no, stage_free = [{}, {}], [{}, {}], [{}, {}], [{}, {}]
        for layer in range(DEPTH):
            turn, staged, free = U0[2 * layer] + 8, B0[2 * layer], None
            for slot, (what, chunk, _, _, _, _, last) in enumerate(plans[layer][0]):
                if last:
                    ends[layer][chunk] = slot
                if not last or what == "out":
                    continue
                leaves[layer][slot + 4] = (what, chunk)
                if what == "v":
                    v_no[layer][chunk] = sum(map(len, v_no))
                    continue
                for pair in range(1 if what == "ki" else 2):
                    after = slot + 2 * pair + (what == "ki")
                    turns[layer][after + 2] = (what, chunk, pair)
                    takes[layer][after + 6] = (what, chunk, pair)
                    turn_no[layer][(chunk, pair)] = turn
                    turn += 1
                if what != "ki":
                    stage_no[layer][chunk] = staged
                    stage_free[layer][chunk] = free
                    free = turn
                    staged += 1
        turn_ki = turn_no[0][(1, 0)]
        idx_lead = 2
        dots_after = {15 + u: u for u in range(6)}
        dots_heads = [(0, 2, 4, 6), (1, 3, 5, 7), (0, 2), (4, 6), (1, 3), (5, 7)]
        dots_tile = [0, 0, 1, 1, 1, 1]
        topk_at = {25 + r: r for r in range(TOPK // 8)}

        def group_of(layer, chunk):
            return (chunk - (idx_lead if layer == 0 else 0)) // 3

        def chunk_of(layer, group, what):
            return 3 * group + "qkv".index(what) + (idx_lead if layer == 0 else 0)

        def heads_before(layer, group):
            per = [8, 8, 4, 4] if layer == 0 else [4] * 4
            return H0[layer] + sum(per[:group + 1])

        def group_head(layer, n):
            per = [8, 8, 4, 4] if layer == 0 else [4] * 4
            return next(g for g in range(4) if n < sum(per[:g + 1]))

        def keys(m):
            return slice(0, P) if m == 0 else slice(P, SC)

        def window(m):
            return slice(P, SEQ) if m == 0 else slice(0, SEQ)

        def x_bank(i):
            return (ps_turn, ps_out, ps_dots, ps_probT)[i % 4]

        def ki_tile(w):
            return w[:].rearrange("p g n -> p (g n)")[:, 0:KB // KT * KI].rearrange("p (g n) -> p g n", n=KI)

        def stick_bank(h):
            return (ps_dots, ps_probT)[stick.index(h) % 2]

        def mlp_tile(mlp, q, c, t):
            return q * (8 * TPC) + (T0[mlp] + (4 + c) * TPC + t)

        block = ctx.enter_context(nc.Block())

        @block.sync
        def _(sp):
            rows = x[0].rearrange("(m p) d -> p m d", p=P)

            def load_x(b):
                cols = slice(b * NC, (b + 1) * NC)
                for m in range(MT):
                    sp.dma_start(X[:, m, cols], rows[:, m, cols]).then_inc(s_x[m][b], 16)

            load_x(0)

            def load(w, tile, j, row, col):
                if not (isinstance(tile, int) and tile < RAW):
                    sp.wait_ge(s_lo, tile - RAW + 1)
                src = w[bass.ds(row, G * P), bass.ds(col, NC)].rearrange("(g p) n -> p g n", p=P)
                sp.dma_start(raw[j % RAW][:], src).then_inc(s_raw[j % RAW], 16)

            def load_ki(tile, t, col):
                sp.wait_ge(s_lo, tile - RAW + 1)
                rows = slice(t * (D // KT), (t + 1) * (D // KT))
                src = even_w_in[0][rows, col:col + KI].rearrange("(g p) n -> p g n", p=P)
                sp.dma_start(ki_tile(raw[tile % RAW]), src).then_inc(s_raw[tile % RAW], 16)

            for layer in range(DEPTH):
                w_in = even_w_in[0] if layer == 0 else odd_w_in[0]
                w_out = even_w_out[0] if layer == 0 else odd_w_out[0]
                for slot, (what, chunk, col, width, t, _, _) in enumerate(plans[layer][0]):
                    tile = T0[2 * layer] + slot
                    if what == "ki":
                        load_ki(tile, t, col)
                    else:
                        load(w_out if what == "out" else w_in, tile, tile, t * G * P, col)
                    if layer == 0 and slot < 3:
                        load_x(slot + 1)

                def chunks(q, cs):
                    for c in cs:
                        for t in range(TPC):
                            tile, j = mlp_tile(2 * layer + 1, q, c, t), mlp_tile(2 * layer + 1, 0, c, t)
                            if c < 4:
                                load(ffn_w2[layer], tile, j, q * D + t * G * P, c * NC)
                            else:
                                load(ffn_w1[layer], tile, j, t * G * P, q * D + (D + (c - 4) * NC))

                chunks(-1, range(4, 8))
                with sp.Fori(0, 3) as q:
                    chunks(q, range(8))
                chunks(3, range(4))
            rows_out = out[0].rearrange("(m p) d -> p m d", p=P)
            for m in range(MT):
                for b in range(4):
                    if m == 1 and b >= 2:
                        sp.wait_ge(s_tail, b - 1)
                    else:
                        sp.wait_ge(s_shifted, 8 * 3 + 4 * m + b + 1)
                    cols = slice(b * NC, (b + 1) * NC)
                    sp.dma_start(rows_out[:, m, cols], X[:, m, cols]).then_inc(s_store, 16)
            sp.wait_ge(s_store, 8 * 16)

        @block.gpsimd
        def _(pool):
            pool.memset(ident[:], 0.0).then_inc(s_const, 1)
            pool.memset(not_before[:], 0.0).then_inc(s_const, 1)
            pool.memset(neg_suffix[:], -1.0).then_inc(s_const, 1)
            pool.memset(neg_ones[:], -1.0).then_inc(s_const, 1)
            pool.memset(minus_half[:], -0.5).then_inc(s_const, 1)
            pool.wait_ge(s_const, 5)
            pool.affine_select(out=ident[:], in_=ident[:], compare_op=ALU.not_equal, fill=1.0, base=0,
                               pattern=[[-1, P]], channel_multiplier=1).then_inc(s_const, 1)
            pool.affine_select(out=not_before[:], in_=not_before[:], compare_op=ALU.is_gt, fill=1.0, base=0,
                               pattern=[[1, P]], channel_multiplier=-1).then_inc(s_const, 1)
            pool.affine_select(out=neg_suffix[:], in_=neg_suffix[:], compare_op=ALU.is_ge, fill=0.0, base=0,
                               pattern=[[-1, P]], channel_multiplier=1).then_inc(s_const, 1)
            pool.dma_start(bucket_sb[:], bucket_rows).then_inc(s_const_in, 16)
            pool.dma_start(table[0:N_BUCKETS, :], rel_bias).then_inc(s_const_in, 16)
            pool.dma_start(counts[:], branch_count).then_inc(s_const_in, 16)
            pool.wait_ge(s_ki, 1)
            pool.dma_start(kiT[DS:2 * DS, :], kiT[0:DS, :]).then_inc(s_ki_copy, 16)
            pool.wait_ge(s_rows_sb, 2)
            pool.dma_start(rows_dram.ap(), bias_rows[:]).then_inc(s_rows_dram, 16)
            pool.wait_ge(s_rows_dram, 16)

            def copy_row(h):
                kind, _, _, row, _, _, _ = all_heads[h]
                k, n, rows = int(kind == DIL), soft.index(h), rows_dram.ap()
                pool.dma_start(copies_dram.ap()[row, k, :, 0:OFF],
                               bass.AP(rows.tensor, (row * 2 + k) * OFF, [[0, P], [1, OFF]]))\
                    .then_inc(s_copies[n % 4], 16)

            def load_bias(h):
                kind, _, _, row, _, _, _ = all_heads[h]
                n = soft.index(h)
                pool.wait_ge(s_copies[n % 4], 16 * (n // 4 + 1))
                if n >= 2:
                    pool.wait_ge(s_nmax, n - 1)
                start = (row * 2 + (kind == DIL)) * P * (OFF + 1) + P - 1
                pool.dma_start(bias[n % 2][:], bass.AP(copies_dram.ap().tensor, start, [[OFF, P], [1, SEQ]]))\
                    .then_inc(s_bias[n % 2], 16)

            def scale_residual(st):
                for m in range(MT):
                    for b in range(4):
                        pool.wait_ge(s_turn, U0[st] + (4 * m + b if st else 2 * b + m) + 1)
                        xb = X[:, m, b * NC:(b + 1) * NC]
                        pool.tensor_scalar(xb, xb, ALPHA, None, ALU.mult).then_inc(s_alpha, 1)

            def norm(n, gains, shifts):
                pool.dma_start(gain[:], bass.AP(gains.tensor, gains.offset, [[0, P], [1, D]])).then_inc(s_gain, 16)
                pool.dma_start(shift[:], bass.AP(shifts.tensor, shifts.offset, [[0, P], [1, D]])).then_inc(s_gain, 16)
                for m in range(MT):
                    pool.wait_ge(s_aggr, 2 * n + m + 1)
                    pool.tensor_scalar(var_eps[:, m:m + 1], mean_var[:, m, 1:2], LN_EPS, None, ALU.add)\
                        .then_inc(s_var, 1)
                    pool.wait_ge(s_var, 2 * n + m + 1)
                    pool.tensor_tensor(rstd[:, m:m + 1], var_eps[:, m:m + 1], minus_half[:, 0:1], ALU.pow)\
                        .then_inc(s_rstd, 1)
                    if m == 0:
                        pool.wait_ge(s_gain, 32 * (n + 1))
                    for b in range(2 if n == 3 and m == 1 else 4):
                        pool.wait_ge(s_scaled, 8 * n + 4 * m + b + 1)
                        xb = X[:, m, b * NC:(b + 1) * NC]
                        pool.tensor_tensor(xb, xb, shift[:, b * NC:(b + 1) * NC], ALU.add).then_inc(s_shifted, 1)

            for layer in range(DEPTH):
                scale_residual(2 * layer)
                own = [h for h in soft if H0[layer] <= h < H0[layer] + len(heads[layer])]
                for h in own[:4]:
                    copy_row(h)
                for h in own[:2]:
                    load_bias(h)
                if layer == 0:
                    for m in range(MT):
                        pool.wait_ge(s_score, N_IDX * (m + 1))
                        pool.affine_select(out=score[:, keys(m)], in_=score[:, keys(m)], compare_op=ALU.is_ge,
                                           fill=NEG, base=m * P, pattern=[[-1, P * (m + 1)]],
                                           channel_multiplier=1).then_inc(s_causal, 1)
                for i in range(2, len(own)):
                    if i + 2 < len(own):
                        copy_row(own[i + 2])
                    load_bias(own[i])
                pool.wait_ge(s_pv, H0[layer] + len(heads[layer]))
                norm(2 * layer, ln_mix_g[layer], ln_mix_b[layer])
                scale_residual(2 * layer + 1)
                mlp = 2 * layer + 1

                with pool.Fori(0, 4) as q:
                    for c in range(4):
                        pool.wait_ge(s_stage, q * 4 + (B0[mlp] + c + 1))
                        pool.wait_ge(s_turn, q * 8 + (U0[mlp] + 8 + 2 * c))
                        pool.tensor_tensor(squared[:], stage[:], stage[:], ALU.mult).then_inc(s_square, 1)
                norm(mlp, ln_ffn_g[layer], ln_ffn_b[layer])

        @block.scalar
        def _(act):
            def high(tile, lap, j):
                act.wait_ge(s_raw[j % RAW], lap)
                if not (isinstance(tile, int) and tile < SPL):
                    act.wait_ge(s_mm, tile - SPL + 1)
                act.activation(whi[j % SPL][:], raw[j % RAW][:], ACT.Copy).then_inc(s_hi, 1)

            def high_at(tile, ki=False):
                if not ki:
                    high(tile, 16 * (tile // RAW + 1), tile)
                    return
                act.wait_ge(s_raw[tile % RAW], 16 * (tile // RAW + 1))
                act.wait_ge(s_mm, tile - SPL + 1)
                act.activation(ki_tile(whi[tile % SPL]), ki_tile(raw[tile % RAW]), ACT.Copy).then_inc(s_hi, 1)

            def turn_high(turn, bank, dst, pair):
                act.wait_ge(s_turn, turn + 1)
                act.activation(dst[:, 2 * pair:2 * pair + 2, :], bank[:].rearrange("p (b t) -> p b t", b=2),
                               ACT.Copy).then_inc(s_turn_hi, 1)

            def turn_high_x(u0, i, m, b):
                act.wait_ge(s_turn, u0 + i + 1)
                act.activation(XTh[:, 4 * b:4 * b + 4, m * P:(m + 1) * P],
                               x_bank(i)[:].rearrange("p (b t) -> p b t", b=4), ACT.Copy).then_inc(s_turn_hi, 1)

            def scaled(n, m, b):
                if b == 0:
                    act.wait_ge(s_rstd, 2 * n + m + 1)
                act.wait_ge(s_gained, 8 * n + 4 * m + b + 1)
                xb = X[:, m, b * NC:(b + 1) * NC]
                act.activation(xb, xb, ACT.Copy, scale=rstd[:, m:m + 1]).then_inc(s_scaled, 1)

            def start():
                for t in range(TPC):
                    if t % 2 == 0:
                        for m in range(MT):
                            turn_high_x(0, t + m, m, t // 2)
                    high_at(t)

            def cross(n):
                tl, tf, u0 = T0[n + 1] - TPC, T0[n + 1], U0[n + 1]
                for t in range(TPC):
                    high_at(tl + t)
                if n < 3:
                    high_at(tf)
                for b in range(4):
                    scaled(n, 0, b)
                if n == 3:
                    for b in range(2):
                        scaled(n, 1, b)
                    return
                for b in range(4):
                    high_at(tf + b + 1)
                    turn_high_x(u0, b, 0, b)
                high_at(tf + 5)
                for b in range(4):
                    scaled(n, 1, b)
                high_at(tf + 6)
                high_at(tf + 7)
                for b in range(4):
                    turn_high_x(u0, 4 + b, 1, b)

            def leave(layer, what, chunk):
                act.wait_ge(s_mm, T0[2 * layer] + ends[layer][chunk] + 1)
                acc = ps[chunk % 2]
                if what == "ki":
                    act.activation(kiT[0:DS, :], acc[0:DS, 0, 0:SEQ], ACT.Copy).then_inc(s_ki, 1)
                    act.activation(wiT[DS:KI, :], acc[DS:KI, 0, 0:SEQ], ACT.Copy).then_inc(s_ki, 1)
                elif what == "v":
                    g = group_of(layer, chunk)
                    if g >= 2:
                        act.wait_ge(s_pv, heads_before(layer, g - 2))
                    if layer == 0 and g == 0:
                        act.wait_ge(s_rows_dram, 16)
                    act.activation(v[g % 2][:], acc[:], ACT.Copy).then_inc(s_v, 1)
                else:
                    sparse = what == "qi" or (layer == 0 and group_of(layer, chunk) < 2)
                    scale = 1.0 if what == "k" else (DS if sparse else DH) ** -0.5
                    if stage_free[layer][chunk] is not None:
                        act.wait_ge(s_turn, stage_free[layer][chunk])
                    act.activation(stage[:], acc[:], ACT.Copy, scale=scale).then_inc(s_stage, 1)

            def relu_dots_of(u):
                act.wait_ge(s_dots, u + 1)
                if u:
                    act.wait_ge(s_score, (0, 4, 8, 10, 12, 14)[u])
                act.activation(relu_dots[:], ps_dots[:], ACT.Relu).then_inc(s_relu, 1)

            def exponentials(h):
                act.wait_ge(s_nmax, soft.index(h) + 1)
                for m in range(MT):
                    lg = logit[h % 2][:, keys(m)]
                    if all_heads[h][0] == DSA:
                        last = act.activation(lg, lg, ACT.Exp, bias=neg_max[:, m:m + 1],
                                              accum_out=den[:, h % 2, m:m + 1])
                    else:
                        last = act.activation(lg, lg, ACT.Exp, bias=neg_max[:, m:m + 1])
                last.then_inc(s_exp, 1)

            def stick_log(h):
                n = stick.index(h)
                act.wait_ge(s_logits, h + 1)
                act.wait_ge(s_right, h - 1)
                act.activation(logit[h % 2][:], stick_bank(h)[:, 0:SC], ACT.Abs).then_inc(s_stick, 1)
                act.wait_ge(s_stick, 3 * n + 1)
                act.activation(logit[h % 2][:], logit[h % 2][:], ACT.Exp, scale=-1.0).then_inc(s_stick, 1)
                act.wait_ge(s_stick, 3 * n + 2)
                act.activation(logit[h % 2][:], logit[h % 2][:], ACT.Ln, bias=1.0).then_inc(s_stick, 1)

            def right_operand(h):
                if h:
                    act.wait_ge(s_pv, h)
                if all_heads[h][0] == SB:
                    act.wait_ge(s_later, stick.index(h) + 1)
                    act.activation(probT[:], stick_bank(h)[:, 0:SC], ACT.Exp).then_inc(s_right, 1)
                else:
                    act.wait_ge(s_probT, soft.index(h) + 1)
                    act.activation(probT[:], ps_probT[:, 0:SC], ACT.Copy).then_inc(s_right, 1)

            def output_high(h):
                kind, _, _, _, blk, part, _ = all_heads[h]
                rows = slice(part, part + (DS if kind == DSA else DH))
                act.wait_ge(s_pv, h + 1)
                act.activation(HTh[rows, blk, :], ps_out[rows, 0:SEQ], ACT.Copy).then_inc(s_ohi, 1)

            start()
            act.wait_ge(s_const, 8)
            act.activation(neg_identr[:], ident[:], ACT.Copy, scale=NEG).then_inc(s_constr, 1)
            for i in range(2):
                act.activation(not_before_r[:, i, :], not_before[:], ACT.Copy).then_inc(s_constr, 1)
            for layer in range(DEPTH):
                t0 = T0[2 * layer]
                plan = plans[layer][0]
                for slot in range(TPC, len(plan) - TPC):
                    high_at(t0 + slot, plan[slot][0] == "ki")
                    if layer == 0 and slot == TPC + KT:
                        act.wait_ge(s_rows, 1)
                        act.activation(bias_rows[:, 0, :], ps_dots[0:16, 0:OFF], ACT.Copy).then_inc(s_rows_sb, 1)
                        act.activation(bias_rows[:, 1, :], ps_probT[0:16, 0:OFF], ACT.Copy).then_inc(s_rows_sb, 1)
                    if slot in leaves[layer]:
                        leave(layer, *leaves[layer][slot])
                    if layer == 0 and slot - 4 in dots_after:
                        relu_dots_of(dots_after[slot - 4])
                    for h in range(H0[layer], H0[layer] + len(heads[layer])):
                        begin = all_heads[h][6]
                        if slot == begin + 4 and all_heads[h][0] == SB:
                            stick_log(h)
                        elif slot == begin + 4:
                            exponentials(h)
                        elif slot == begin + 7:
                            right_operand(h)
                        elif slot == begin + 9:
                            output_high(h)
                mlp = 2 * layer + 1
                cross(2 * layer)

                def chunks(q, cs):
                    for c in cs:
                        relu = 4 * q + (3 if c == 0 else c - 1)
                        for t in range(TPC):
                            tile = mlp_tile(mlp, q, c, t)
                            j = mlp_tile(mlp, 0, c, t)
                            high(tile, q * (8 * TPC * 16 // RAW) + 16 * (j // RAW + 1), j)
                            if 1 <= c <= 4:
                                continue
                            if t == 3:
                                act.wait_ge(s_mm, mlp_tile(mlp, q, c, 0))
                                if not (isinstance(relu, int) and 16 * layer + relu == 0):
                                    act.wait_ge(s_square, relu + 16 * layer)
                                act.activation(stage[:], ps[(c - 1) % 2][:], ACT.Relu).then_inc(s_stage, 1)
                            if t in (6, 7):
                                pair = (6 if c == 0 else 2 * (c - 5)) + t - 6
                                turn = (8 * q if c == 0 else 8 * q + 8) + (U0[mlp] + 8 + pair)
                                turn_high(turn, (ps_turn, ps_out)[t - 6], HTh, pair)

                chunks(-1, range(5, 8))
                with act.Fori(0, 3) as q:
                    chunks(q, range(8))
                chunks(3, range(3))
                cross(mlp)

        @block.vector
        def _(dve):
            dve.memset(table[N_BUCKETS:N_BUCKETS + 1, :], 1.0).then_inc(s_one, 1)

            def low(tile, j, ki=False):
                dve.wait_ge(s_hi, tile + 1)
                if not (isinstance(tile, int) and tile < SPL):
                    dve.wait_ge(s_mm, tile - SPL + 1)
                if ki:
                    dve.tensor_tensor(ki_tile(wlo[j % SPL]), ki_tile(raw[j % RAW]),
                                      ki_tile(whi[j % SPL]).bitcast(F32), ALU.subtract).then_inc(s_lo, 1)
                else:
                    dve.tensor_tensor(wlo[j % SPL][:], raw[j % RAW][:], whi[j % SPL][:].bitcast(F32),
                                      ALU.subtract).then_inc(s_lo, 1)

            def turn_low(turn_hi, bank, hi, lo, pair):
                dve.wait_ge(s_turn_hi, turn_hi + 1)
                dve.tensor_tensor(lo[:, 2 * pair:2 * pair + 2, :], bank[:].rearrange("p (b t) -> p b t", b=2),
                                  hi[:, 2 * pair:2 * pair + 2, :].bitcast(F32), ALU.subtract).then_inc(s_turned, 1)

            def turn_low_x(h0, i, m, b):
                dve.wait_ge(s_turn_hi, h0 + i + 1)
                part = (slice(None), slice(4 * b, 4 * b + 4), slice(m * P, (m + 1) * P))
                dve.tensor_tensor(XTl[part], x_bank(i)[:].rearrange("p (b t) -> p b t", b=4),
                                  XTh[part].bitcast(F32), ALU.subtract).then_inc(s_turned, 1)

            def add(st, c, done):
                dve.wait_ge(s_mm, done)
                dve.wait_ge(s_alpha, 8 * st + 8)
                xb = X[:, :, c * NC:(c + 1) * NC]
                dve.tensor_tensor(xb, ps[c % 2][:], xb, ALU.add).then_inc(s_added, 1)

            def statistics(n, c):
                dve.wait_ge(s_added, n + 1)
                for m in range(MT):
                    last = dve.bn_stats(stats[:, m, c, :], X[:, m, c * NC:(c + 1) * NC])
                last.then_inc(s_stat, 1)

            def last_chunk(n, m):
                if m == 0:
                    dve.wait_ge(s_half, n + 1)
                else:
                    dve.wait_ge(s_mm, T0[n + 1])
                xb = X[:, m, 3 * NC:D]
                dve.tensor_tensor(xb, ps[1][:, m, :], xb, ALU.add).then_inc(s_last, 1)
                dve.wait_ge(s_last, 2 * n + m + 1)
                dve.bn_stats(stats[:, m, 3, :], xb).then_inc(s_stat, 1)
                dve.wait_ge(s_stat, V0[n + 1] + 2 * n + m + 1)
                dve.bn_aggr(mean_var[:, m, :], stats[:, m, :, :]).then_inc(s_aggr, 1)

            def gained(n, m, b):
                if b == 0:
                    dve.wait_ge(s_aggr, 2 * n + m + 1)
                if m == b == 0:
                    dve.wait_ge(s_gain, 32 * (n + 1))
                xb = X[:, m, b * NC:(b + 1) * NC]
                dve.scalar_tensor_tensor(out=xb, in0=xb, scalar=mean_var[:, m, 0:1], in1=gain[:, b * NC:(b + 1) * NC],
                                         op0=ALU.subtract, op1=ALU.mult).then_inc(s_gained, 1)

            def hi_count(st):
                return sum((8, 40)[i % 2] for i in range(st))

            def start():
                for t in range(TPC):
                    if t % 2 == 0:
                        for m in range(MT):
                            turn_low_x(0, t + m, m, t // 2)
                    low(t, t)

            def cross(n):
                tl, tf, h0 = T0[n + 1] - TPC, T0[n + 1], hi_count(n + 1)
                for t in range(TPC):
                    low(tl + t, tl + t)
                    if t == 3:
                        add(n, 2, tl)
                    if t == 4:
                        statistics(V0[n + 1] - 1, 2)
                last_chunk(n, 0)
                for b in range(4):
                    gained(n, 0, b)
                if n == 3:
                    last_chunk(n, 1)
                    for b in range(4):
                        gained(n, 1, b)
                    dve.wait_ge(s_rstd, 2 * n + 2)
                    for b in range(2, 4):
                        dve.wait_ge(s_gained, 8 * n + 4 + b + 1)
                        xb = X[:, 1, b * NC:(b + 1) * NC]
                        dve.scalar_tensor_tensor(out=xb, in0=xb, scalar=rstd[:, 1:2],
                                                 in1=shift[:, b * NC:(b + 1) * NC],
                                                 op0=ALU.mult, op1=ALU.add).then_inc(s_tail, 1)
                    return
                low(tf, tf)
                for b in range(3):
                    low(tf + b + 1, tf + b + 1)
                    turn_low_x(h0, b, 0, b)
                low(tf + 4, tf + 4)
                last_chunk(n, 1)
                for b in range(4):
                    gained(n, 1, b)
                low(tf + 5, tf + 5)
                turn_low_x(h0, 3, 0, 3)
                low(tf + 6, tf + 6)
                low(tf + 7, tf + 7)
                for b in range(4):
                    turn_low_x(h0, 4 + b, 1, b)

            def take(layer, what, chunk, pair):
                turn = turn_no[layer][(chunk, pair)]
                dve.wait_ge(s_turn, turn + 1)
                if what == "q" and layer == 0:
                    dve.wait_ge(s_rows, 1)
                if what == "ki":
                    dve.tensor_scalar(wi[:], ps_turn[:, 0:MT * N_IDX].rearrange("p (m n) -> p m n", m=MT),
                                      N_IDX ** -0.5, None, ALU.mult).then_inc(s_turned, 1)
                    return
                if what == "qi":
                    dst = qiT
                else:
                    g = group_of(layer, chunk)
                    dst = (qT if what == "q" else kT)[g % 2]
                    if g >= 2:
                        dve.wait_ge(s_logits, heads_before(layer, g - 2))
                dve.tensor_copy(dst[:, 2 * pair:2 * pair + 2, :],
                                ps_turn[:].rearrange("p (b t) -> p b t", b=2)).then_inc(s_turned, 1)

            def score_terms(u):
                m, hs = dots_tile[u], dots_heads[u]
                dve.wait_ge(s_relu, u + 1)
                dve.wait_ge(s_turned, turn_ki + 1)
                width = P * (m + 1)
                for i, h in enumerate(hs):
                    n = (0, 4, 8, 10, 12, 14)[u] + i
                    term = relu_dots[:, i * width:(i + 1) * width]
                    if n % N_IDX == 0:
                        dve.tensor_scalar(score[:, keys(m)], term, wi[:, m, h:h + 1], None, ALU.mult)\
                            .then_inc(s_score, 1)
                        continue
                    dve.wait_ge(s_score, n)
                    dve.scalar_tensor_tensor(out=score[:, keys(m)], in0=term, scalar=wi[:, m, h:h + 1],
                                             in1=score[:, keys(m)], op0=ALU.mult, op1=ALU.add).then_inc(s_score, 1)

            def topk_round(r):
                src = score if r == 0 else work
                if r == 0:
                    dve.wait_ge(s_causal, MT)
                else:
                    dve.wait_ge(s_top, 4 * r)
                for m in range(MT):
                    dve.max(top8[:, m, :], src[:, keys(m)]).then_inc(s_top, 1)
                for m in range(MT):
                    dve.wait_ge(s_top, 4 * r + m + 1)
                    dve.match_replace(work[:, keys(m)], top8[:, m, :], src[:, keys(m)], LOWEST).then_inc(s_top, 1)

            def selection():
                dve.wait_ge(s_top, 4 * (TOPK // 8))
                dve.tensor_tensor(unpicked[:], work[:], score[:], ALU.is_equal).then_inc(s_pick, 1)

            def masked_bias(h):
                n = soft.index(h)
                dve.wait_ge(s_pick, 1)
                dve.wait_ge(s_bias[n % 2], 16 * (n // 2 + 1))
                if h >= 2:
                    dve.wait_ge(s_right, h - 1)
                for m in range(MT):
                    last = dve.scalar_tensor_tensor(out=logit[h % 2][:, keys(m)], in0=unpicked[:, keys(m)], scalar=NEG,
                                                    in1=bias[n % 2][:, window(m)], op0=ALU.mult, op1=ALU.add)
                last.then_inc(s_masked, 1)

            def logits_max(h):
                n = soft.index(h)
                dve.wait_ge(s_logits, h + 1)
                if all_heads[h][0] == DSA:
                    dve.wait_ge(s_masked, h + 1)
                else:
                    dve.wait_ge(s_bias[n % 2], 16 * (n // 2 + 1))
                    dve.wait_ge(s_right, h - 1)
                for m in range(MT):
                    added = logit[h % 2][:, keys(m)] if all_heads[h][0] == DSA else bias[n % 2][:, window(m)]
                    last = dve.tensor_tensor_reduce(
                        out=logit[h % 2][:, keys(m)], in0=ps_dots[:, keys(m)], in1=added,
                        scale=1.0, scalar=LOWEST, op0=ALU.add, op1=ALU.max, accum_out=row_max[:, m:m + 1])
                last.then_inc(s_max, 1)
                dve.wait_ge(s_max, n + 1)
                if n:
                    dve.wait_ge(s_exp, n)
                dve.tensor_scalar(neg_max[:], row_max[:], -1.0, None, ALU.mult).then_inc(s_nmax, 1)

            def probabilities(h):
                n = soft.index(h)
                dve.wait_ge(s_exp, n + 1)
                if n >= 2:
                    dve.wait_ge(s_probT, n - 1)
                src = logit[h % 2]
                if all_heads[h][0] == DIL:
                    d = dilated.index(h)
                    for m in range(MT):
                        last = dve.tensor_tensor_reduce(
                            out=prob[h % 2][:, keys(m)], in0=src[:, keys(m)], in1=counts[:, window(m)],
                            scale=1.0, scalar=0.0, op0=ALU.mult, op1=ALU.add, accum_out=den[:, h % 2, m:m + 1])
                    last.then_inc(s_den, 1)
                    dve.wait_ge(s_den, d + 1)
                    src = prob[h % 2]
                dve.reciprocal(rden[:], den[:, h % 2, :]).then_inc(s_rden, 1)
                dve.wait_ge(s_rden, n + 1)
                for m in range(MT):
                    last = dve.tensor_scalar(prob[h % 2][:, keys(m)], src[:, keys(m)], rden[:, m:m + 1], None, ALU.mult)
                last.then_inc(s_prob, 1)

            def softplus(h):
                n = stick.index(h)
                dve.wait_ge(s_stick, 3 * n + 3)
                if n < 2:
                    dve.wait_ge(s_probT, 16)
                else:
                    dve.wait_ge(s_later, n - 1)
                dve.scalar_tensor_tensor(out=prob[h % 2][:], in0=stick_bank(h)[:, 0:SC], scalar=0.0,
                                         in1=logit[h % 2][:], op0=ALU.max, op1=ALU.add).then_inc(s_keep, 1)

            def output_low(h):
                kind, _, _, _, blk, part, _ = all_heads[h]
                rows = slice(part, part + (DS if kind == DSA else DH))
                dve.wait_ge(s_ohi, h + 1)
                dve.tensor_tensor(HTl[rows, blk, :], ps_out[rows, 0:SEQ], HTh[rows, blk, :].bitcast(F32),
                                  ALU.subtract).then_inc(s_olo, 1)

            start()
            for layer in range(DEPTH):
                st = 2 * layer
                plan, n_in = plans[layer]
                for slot in range(TPC, len(plan) - TPC):
                    low(T0[st] + slot, T0[st] + slot, plan[slot][0] == "ki")
                    if slot in takes[layer]:
                        take(layer, *takes[layer][slot])
                    if layer == 0 and slot - 4 in dots_after:
                        score_terms(dots_after[slot - 4])
                    if layer == 0 and slot in topk_at:
                        topk_round(topk_at[slot])
                    if layer == 0 and slot == max(topk_at) + 1:
                        selection()
                    for h in range(H0[layer], H0[layer] + len(heads[layer])):
                        begin = all_heads[h][6]
                        if slot == begin + 2 and all_heads[h][0] == DSA:
                            masked_bias(h)
                        elif slot == begin + 4 and all_heads[h][0] != SB:
                            logits_max(h)
                        elif slot == begin + 5 and all_heads[h][0] == SB:
                            softplus(h)
                        elif slot == begin + 5:
                            probabilities(h)
                        elif slot == begin + 9:
                            output_low(h)
                    for c in range(2):
                        if slot == ends[layer][n_in + c] + 4:
                            add(st, c, T0[st] + ends[layer][n_in + c] + 1)
                        if slot == ends[layer][n_in + c] + 5:
                            statistics(V0[st] + c, c)
                mlp = st + 1
                cross(st)

                def chunks(q, cs):
                    for c in cs:
                        for t in range(TPC):
                            low(mlp_tile(mlp, q, c, t), mlp_tile(mlp, 0, c, t))
                            if not 1 <= c <= 4 and t in (6, 7):
                                pair = (6 if c == 0 else 2 * (c - 5)) + t - 6
                                taken = (8 * q if c == 0 else 8 * q + 8) + (hi_count(mlp) + 8 + pair)
                                turn_low(taken, (ps_turn, ps_out)[t - 6], HTh, HTl, pair)
                            if 1 <= c <= 4 and t == 3:
                                add(mlp, c - 1, mlp_tile(mlp, q, c, 0))
                            if 1 <= c <= 4 and t == 4:
                                statistics(q * 4 + (V0[mlp] + c - 1), c - 1)

                chunks(-1, range(5, 8))
                with dve.Fori(0, 3) as q:
                    chunks(q, range(8))
                chunks(3, range(3))
                cross(mlp)

        @block.tensor
        def _(pe):
            def multiply(tile, j, acc, hi, lo, t, first, last, tokens=range(MT), half=False):
                pe.wait_ge(s_lo, tile + 1)
                for g in range(G):
                    k = G * t + g
                    for m in tokens:
                        dst = acc[:, m, :]
                        wh, wl = whi[j % SPL][:, g, :], wlo[j % SPL][:, g, :]
                        xh, xl = hi[:, k, m * P:(m + 1) * P], lo[:, k, m * P:(m + 1) * P]
                        pe.matmul(dst, xl, wh, start=first and g == 0, stop=False)
                        pe.matmul(dst, xh, wl, start=False, stop=False)
                        mm = pe.matmul(dst, xh, wh, start=False, stop=last and g == G - 1)
                if MT - 1 in tokens:
                    mm.then_inc(s_mm, 1)
                elif last and half:
                    mm.then_inc(s_half, 1)

            def multiply_ki(tile, t, acc):
                pe.wait_ge(s_lo, tile + 1)
                wh, wl, dst = ki_tile(whi[tile % SPL]), ki_tile(wlo[tile % SPL]), acc[0:KI, 0, 0:SEQ]
                for g in range(KB // KT):
                    k = KB // KT * t + g
                    pe.matmul(dst, wl[:, g, :], XTh[:, k, :], start=k == 0, stop=False)
                    pe.matmul(dst, wh[:, g, :], XTl[:, k, :], start=False, stop=False)
                    mm = pe.matmul(dst, wh[:, g, :], XTh[:, k, :], start=False, stop=k == KB - 1)
                mm.then_inc(s_mm, 1)

            def turn_pair(turn, bank, src, pair, lag=0):
                if not (isinstance(turn, int) and turn - lag < 1):
                    pe.wait_ge(s_turned, turn - lag)
                for b in range(2):
                    for m in range(MT):
                        col = (2 * pair + b) * P
                        last = pe.transpose(bank[:, (b * MT + m) * P:(b * MT + m + 1) * P], src[:, m, col:col + P],
                                            ident[:])
                last.then_inc(s_turn, 1)

            def turn_x(u0, i, m, b):
                if u0 or i >= 4:
                    pe.wait_ge(s_turned, u0 + max(i - 3, 0))
                for k in range(4):
                    last = pe.transpose(x_bank(i)[:, k * P:(k + 1) * P], X[:, m, (4 * b + k) * P:(4 * b + k + 1) * P],
                                        ident[:])
                last.then_inc(s_turn, 1)

            def start():
                pe.wait_ge(s_const, 6)
                for t in range(TPC):
                    if t % 2 == 0:
                        for b in range(2) if t == 0 else range(t // 2 + 1, min(t // 2 + 2, 4)):
                            for m in range(MT):
                                pe.wait_ge(s_x[m][b], 16)
                                turn_x(0, 2 * b + m, m, b)
                    for m in range(MT):
                        pe.wait_ge(s_turned, 2 * (t // 2) + m + 1)
                        multiply(t, t, ps[0], XTh, XTl, t, t == 0, t == TPC - 1, tokens=(m,))
                pe.wait_ge(s_const_in, 48)
                pe.wait_ge(s_const, 8)
                pe.wait_ge(s_one, 1)
                pe.matmul(ps_dots[0:16, 0:OFF], table[:], bucket_sb[:, 0, :], start=True, stop=True)
                pe.matmul(ps_probT[0:16, 0:OFF], table[:], bucket_sb[:, 1, :], start=True,
                          stop=True).then_inc(s_rows, 1)

            def cross(n, t_of_slot):
                tl, tf, u0 = T0[n + 1] - TPC, T0[n + 1], U0[n + 1]

                def normed(m, b):
                    pe.wait_ge(s_shifted, 8 * n + 4 * m + b + 1)
                    turn_x(u0, 4 * m + b, m, b)

                for i, t in enumerate(t_of_slot):
                    multiply(tl + i, tl + i, ps[1], HTh, HTl, t, i == 0, i == TPC - 1, tokens=(0,), half=True)
                for i, t in enumerate(t_of_slot):
                    multiply(tl + i, tl + i, ps[1], HTh, HTl, t, i == 0, i == TPC - 1, tokens=(1,))
                    if n < 3 and 3 <= i < 7:
                        normed(0, i - 3)
                if n == 3:
                    return
                pe.wait_ge(s_added, V0[n + 1])
                for m in range(MT):
                    for t in range(TPC):
                        pe.wait_ge(s_turned, u0 + 4 * m + t // 2 + 1)
                        multiply(tf + t, tf + t, ps[0], XTh, XTl, t, t == 0, t == TPC - 1, tokens=(m,))
                        if m == 0 and t >= 4:
                            normed(1, t - 4)

            def free(layer, chunk):
                what = next(w for w, c, *_ in plans[layer][0] if c == chunk)
                if what == "ki":
                    pe.wait_ge(s_ki, 2)
                elif what == "v":
                    pe.wait_ge(s_v, v_no[layer][chunk] + 1)
                elif what == "out":
                    pe.wait_ge(s_added, V0[2 * layer] + chunk - plans[layer][1] + 1)
                else:
                    pe.wait_ge(s_stage, stage_no[layer][chunk] + 1)

            def turn_chunk(layer, what, chunk, pair):
                turn = turn_no[layer][(chunk, pair)]
                if what == "ki":
                    pe.wait_ge(s_ki, 2)
                    pe.wait_ge(s_turned, turn)
                    for m in range(MT):
                        last = pe.transpose(ps_turn[:, m * N_IDX:(m + 1) * N_IDX], wiT[DS:KI, m * P:(m + 1) * P],
                                            ident[DS:KI, DS:KI])
                    last.then_inc(s_turn, 1)
                    return
                pe.wait_ge(s_stage, stage_no[layer][chunk] + 1)
                turn_pair(turn, ps_turn, stage, pair)

            def dots(u):
                m, hs = dots_tile[u], dots_heads[u]
                width = P * (m + 1)
                pe.wait_ge(s_turned, turn_ki + 1)
                pe.wait_ge(s_ki_copy, 16)
                pe.wait_ge(s_rows_sb, 2) if u == 0 else pe.wait_ge(s_relu, u)
                for i, h in enumerate(hs):
                    rows = slice((h % 2) * DS, (h % 2 + 1) * DS)
                    last = pe.matmul(ps_dots[:, i * width:(i + 1) * width], qiT[rows, h // 2, m * P:(m + 1) * P],
                                     kiT[rows, 0:width], start=i == 0, stop=i == len(hs) - 1, skip_group_check=True)
                last.then_inc(s_dots, 1)

            def head_scores(layer, h):
                kind, parity, i, _, _, _, _ = all_heads[h]
                g = group_head(layer, h - H0[layer])
                pe.wait_ge(s_turned, turn_no[layer][(chunk_of(layer, g, "k"), 1)] + 1)
                if kind == SB:
                    n = stick.index(h)
                    if n == 0:
                        pe.wait_ge(s_nmax, 16)
                    pe.wait_ge(s_right, h - 1)
                    pe.wait_ge(s_constr, 3)
                    bank = stick_bank(h)
                    q, k = qT[parity][:, i, :], kT[parity][:, i, :]
                    pe.matmul(bank[:, 0:SEQ], k[:, 0:P], q, start=True, stop=False, skip_group_check=True)
                    pe.matmul(bank[:, SEQ:SC], k[:, P:SEQ], q[:, P:SEQ], start=False, stop=False, skip_group_check=True)
                    pe.matmul(bank[:].rearrange("p (a t) -> p a t", a=2)[:, :, 0:P], neg_identr[:], not_before_r[:],
                              start=False, stop=True, skip_group_check=True).then_inc(s_logits, 1)
                    return
                n = soft.index(h)
                if h == 0:
                    pe.wait_ge(s_relu, 6)
                elif h == H0[1]:
                    pe.wait_ge(s_right, h)
                else:
                    pe.wait_ge(s_nmax, n)
                if kind == DSA:
                    rows, blk = slice((i % 2) * DS, (i % 2 + 1) * DS), i // 2
                else:
                    rows, blk = slice(0, P), i
                q, k = qT[parity][rows, blk, :], kT[parity][rows, blk, :]
                for m in range(MT):
                    last = pe.matmul(ps_dots[:, keys(m)], q[:, m * P:(m + 1) * P], k[:, 0:P * (m + 1)],
                                     start=m == 0, stop=m == 1, skip_group_check=True)
                last.then_inc(s_logits, 1)

            def head_turn(h):
                pe.wait_ge(s_prob, soft.index(h) + 1)
                if h:
                    pe.wait_ge(s_right, h)
                p = prob[h % 2]
                pe.transpose(ps_probT[:, 0:P], p[:, 0:P], ident[:])
                pe.transpose(ps_probT[:, P:SEQ], p[:, P:SEQ], ident[:])
                pe.transpose(ps_probT[:, SEQ:SC], p[:, SEQ:SC], ident[:]).then_inc(s_probT, 1)

            def stick_sum(h):
                pe.wait_ge(s_keep, stick.index(h) + 1)
                bank, sp_ = stick_bank(h), prob[h % 2]
                pe.matmul(bank[:, 0:SEQ], neg_suffix[:], sp_[:, 0:SEQ], start=False, stop=False, skip_group_check=True)
                pe.matmul(bank[:, P:SEQ], neg_ones[:], sp_[:, SEQ:SC], start=False, stop=False, skip_group_check=True)
                pe.matmul(bank[:, SEQ:SC], neg_suffix[:], sp_[:, SEQ:SC], start=False, stop=True,
                          skip_group_check=True).then_inc(s_later, 1)

            def head_output(layer, h):
                kind, parity, i, _, _, part, _ = all_heads[h]
                g = group_head(layer, h - H0[layer])
                width = DS if kind == DSA else DH
                pe.wait_ge(s_v, v_no[layer][chunk_of(layer, g, "v")] + 1)
                pe.wait_ge(s_right, h + 1)
                if h:
                    pe.wait_ge(s_olo, h)
                cols = slice(i * width, (i + 1) * width)
                dst = ps_out[part:part + width, :]
                pe.matmul(dst[:, 0:SEQ], v[parity][:, 0, cols], probT[:, 0:SEQ], start=True, stop=False)
                pe.matmul(dst[:, P:SEQ], v[parity][:, 1, cols], probT[:, SEQ:SC], start=False,
                          stop=True).then_inc(s_pv, 1)

            start()
            for layer in range(DEPTH):
                st = 2 * layer
                plan, n_in = plans[layer]
                for slot in range(TPC, len(plan) - TPC):
                    what, chunk, _, _, t, first, last = plan[slot]
                    tile = T0[st] + slot
                    if first:
                        if chunk >= 2:
                            free(layer, chunk - 2)
                        elif st:
                            pe.wait_ge(s_last, 2 * st)
                    if what == "out":
                        done = max(h for h in range(H0[layer], H0[layer] + len(heads[layer]))
                                   if all_heads[h][4] // G == t)
                        pe.wait_ge(s_olo, done + 1)
                        multiply(tile, tile, ps[chunk % 2], HTh, HTl, t, first, last)
                    elif what == "ki":
                        multiply_ki(tile, t, ps[chunk % 2])
                    else:
                        multiply(tile, tile, ps[chunk % 2], XTh, XTl, t, first, last)
                    if slot in turns[layer]:
                        turn_chunk(layer, *turns[layer][slot])
                    if layer == 0 and slot in dots_after:
                        dots(dots_after[slot])
                    for h in range(H0[layer], H0[layer] + len(heads[layer])):
                        begin = all_heads[h][6]
                        if slot == begin:
                            head_scores(layer, h)
                        elif slot == begin + 3 and all_heads[h][0] == SB:
                            stick_sum(h)
                        elif slot == begin + 3:
                            head_turn(h)
                        elif slot == begin + 5:
                            head_output(layer, h)
                mlp = st + 1
                free(layer, n_in + 1)
                cross(st, [s[4] for s in plan[-TPC:]])

                def chunks(q, cs):
                    for c in cs:
                        if c == 5 and isinstance(q, int):
                            pe.wait_ge(s_last, 2 * mlp)
                        elif c in (0, 1):
                            pe.wait_ge(s_stage, q * 4 + (B0[mlp] + c + 3))
                        elif c <= 5:
                            pe.wait_ge(s_added, q * 4 + (V0[mlp] + c - 1))
                        else:
                            pe.wait_ge(s_stage, q * 4 + (B0[mlp] + c - 1))
                        hi, lo = (HTh, HTl) if c < 4 else (XTh, XTl)
                        for t in range(TPC):
                            if c == 0:
                                pe.wait_ge(s_turned, q * 8 + (U0[mlp] + 8 + t + 1))
                            multiply(mlp_tile(mlp, q, c, t), mlp_tile(mlp, 0, c, t), ps[c % 2], hi, lo, t,
                                     t == 0, t == TPC - 1)
                            if not 1 <= c <= 4 and t in (2, 3):
                                pair = (6 if c == 0 else 2 * (c - 5)) + t - 2
                                if t == 2:
                                    pe.wait_ge(s_square, q * 4 + (16 * layer + (4 if c == 0 else c)))
                                turn_pair((8 * q if c == 0 else 8 * q + 8) + (U0[mlp] + 8 + pair),
                                          (ps_turn, ps_out)[t - 2], squared, t - 2, lag=1)

                chunks(-1, range(5, 8))
                with pe.Fori(0, 3) as q:
                    chunks(q, range(8))
                chunks(3, range(3))
                pe.wait_ge(s_added, V0[mlp] + 14)
                cross(mlp, range(TPC))


_INS = ["x", "even_w_in", "even_w_out", "odd_w_in", "odd_w_out", "rel_bias", "ln_mix_g", "ln_mix_b",
        "ffn_w1", "ffn_w2", "ln_ffn_g", "ln_ffn_b"]


def shape_constants():
    dist = SEQ - 1 - np.arange(OFF)
    back = np.maximum(dist, 0)
    exact = N_BUCKETS // 2
    large = exact + (np.log(np.maximum(back, 1).astype(np.float32) / np.float32(exact))
                     / np.float32(np.log(BUCKET_MAX_DIST / exact)) * np.float32(N_BUCKETS - exact)).astype(np.int32)
    bucket = np.where(back < exact, back, np.minimum(large, N_BUCKETS - 1))
    reach = np.zeros(OFF, np.float32)
    for window, dilation in CONFIGS:
        reach += (dist >= 0) & (dist % dilation == 0) & (dist // dilation <= window // dilation)
    rows = np.zeros((N_BUCKETS + 1, 2, OFF), np.float32)
    rows[bucket, :, np.arange(OFF)] = 1.0
    rows[N_BUCKETS, 0] = np.where(dist >= 0, 0.0, NEG)
    rows[N_BUCKETS, 1] = np.where(reach > 0, 0.0, NEG)
    t, s = np.arange(P)[:, None], np.arange(SEQ)[None, :]
    return {"bucket_rows": rows, "branch_count": reach[SEQ - 1 - (t + P - s)]}


def kernel(**inputs):
    import concourse.bacc as _bacc
    from concourse.bass_utils import run_bass_kernel_spmd as _run

    nc = _bacc.Bacc("TRN2", target_bir_lowering=False, num_devices=1)
    arrays, args = {}, []
    for name, a in [(n, inputs[n]) for n in _INS] + list(shape_constants().items()):
        a = np.ascontiguousarray(a)
        arrays[f"in_{name}_dram"] = a
        args.append(nc.dram_tensor(f"in_{name}_dram", a.shape, mybir.dt.from_np(a.dtype), kind="ExternalInput").ap())
    args.append(nc.dram_tensor("out_0_dram", (1, SEQ, D), F32, kind="ExternalOutput").ap())
    hybrid_trunk(nc, *args)
    r = _run(nc, [arrays], core_ids=[0])
    return r.results[0]["out_0_dram"]
```
